# Optimizing a Trainium2 kernel written in Bass

```python
import math, functools
import jax, jax.numpy as jnp
from jax import lax
import numpy as np

D_MODEL = 1024
BATCH = 1
SEQ = 512
DEPTH = 2
DEC_BATCH = 8
DEC_SEQ = 8
PAST_LEN = 256
PAGE_SIZE = 128

N_A = DEPTH // 2
N_B = DEPTH - N_A
D_FF = ((8 * D_MODEL // 3 + 127) // 128) * 128
P_DIM = 256
H_A = 8
DK = 128
DV = 128
QKV_DIM = H_A * (2 * DK + DV)
PROJ_A = QKV_DIM + H_A * DV + 2 * H_A
CONV_W = 4
CHUNK = 64
H_B = 16
HD_B = D_MODEL // H_B
Q_BLOCK = 128
SB_BIAS_INIT = -8.0
EPS = 1e-6

kernel_name = "yoco_gdn_stickbreaking_macaron_step"

def _rms_norm(x, g):
    xf = x.astype(jnp.float32)
    y = xf * lax.rsqrt(jnp.mean(xf * xf, axis=-1, keepdims=True) + EPS)
    return (y * g.astype(jnp.float32)).astype(x.dtype)

def _l2norm(x):
    return x * lax.rsqrt(jnp.sum(x * x, axis=-1, keepdims=True) + EPS)

def _swiglu(h, w_in, w_out):
    gu = h @ w_in
    gate, up = gu[..., :D_FF], gu[..., D_FF:]
    return (jax.nn.silu(gate) * up) @ w_out

def _gated_delta_chunked(q, k, v, g, beta, s0):
    f32 = jnp.float32
    bsz, t_len, h, dk = q.shape
    dv = v.shape[-1]
    c = min(CHUNK, t_len)
    pad = (-t_len) % c
    q = _l2norm(q.astype(f32)) * (dk ** -0.5)
    k = _l2norm(k.astype(f32))
    v = v.astype(f32)
    g = g.astype(f32)
    beta = beta.astype(f32)
    if pad:
        pw = ((0, 0), (0, pad), (0, 0), (0, 0))
        q, k, v = jnp.pad(q, pw), jnp.pad(k, pw), jnp.pad(v, pw)
        g, beta = jnp.pad(g, pw[:3]), jnp.pad(beta, pw[:3])
    n = (t_len + pad) // c

    def blk(t):
        return jnp.moveaxis(t.reshape((bsz, n, c, h) + t.shape[3:]), 3, 1)

    q, k, v, g, beta = blk(q), blk(k), blk(v), blk(g), blk(beta)
    gc = jnp.cumsum(g, axis=-1)
    incl = jnp.tril(jnp.ones((c, c), dtype=bool))
    strict = jnp.tril(jnp.ones((c, c), dtype=bool), -1)
    diff = gc[..., :, None] - gc[..., None, :]
    decay = jnp.where(incl, jnp.exp(jnp.where(incl, diff, 0.0)), 0.0)
    kb = k * beta[..., None]
    m = jnp.where(strict, jnp.einsum('bhnid,bhnjd->bhnij', kb, k) * decay, 0.0)
    eye = jnp.eye(c, dtype=f32)
    rhs = jnp.concatenate([v * beta[..., None], kb * jnp.exp(gc)[..., None]], axis=-1)
    sol = lax.linalg.triangular_solve(eye + m, rhs, left_side=True, lower=True,
                                      unit_diagonal=True)
    u, w = sol[..., :dv], sol[..., dv:]
    qk = jnp.where(incl, jnp.einsum('bhnid,bhnjd->bhnij', q, k) * decay, 0.0)
    q_dec = q * jnp.exp(gc)[..., None]
    k_dec = k * jnp.exp(gc[..., -1:] - gc)[..., None]
    g_tot = jnp.exp(gc[..., -1])

    def step(s, xs):
        u_n, w_n, qk_n, qd_n, kd_n, gt_n = xs
        v_new = u_n - jnp.einsum('bhck,bhkv->bhcv', w_n, s)
        o_n = (jnp.einsum('bhck,bhkv->bhcv', qd_n, s)
               + jnp.einsum('bhcs,bhsv->bhcv', qk_n, v_new))
        s = s * gt_n[..., None, None] + jnp.einsum('bhck,bhcv->bhkv', kd_n, v_new)
        return s, o_n

    xs = tuple(jnp.moveaxis(t, 2, 0) for t in (u, w, qk, q_dec, k_dec, g_tot))
    s_fin, o = lax.scan(step, s0.astype(f32), xs)
    o = jnp.moveaxis(jnp.moveaxis(o, 0, 2), 1, 3).reshape(bsz, n * c, h, dv)[:, :t_len]
    return o, s_fin

def _gdn_mixer(h, conv_prev, s0, w_in, w_conv, a_log, dt_bias, o_norm, w_out):
    bsz, t_len, _ = h.shape
    proj = h @ w_in
    qkv = proj[..., :QKV_DIM]
    gate = proj[..., QKV_DIM:QKV_DIM + H_A * DV]
    a_in = proj[..., QKV_DIM + H_A * DV:QKV_DIM + H_A * DV + H_A]
    b_in = proj[..., QKV_DIM + H_A * DV + H_A:]
    xp = jnp.concatenate([conv_prev.astype(qkv.dtype), qkv], axis=1)
    conv = xp[:, 0:t_len] * w_conv[0]
    for j in range(1, CONV_W):
        conv = conv + xp[:, j:j + t_len] * w_conv[j]
    conv = jax.nn.silu(conv)
    new_conv = xp[:, t_len:]
    q = conv[..., :H_A * DK].reshape(bsz, t_len, H_A, DK)
    k = conv[..., H_A * DK:2 * H_A * DK].reshape(bsz, t_len, H_A, DK)
    v = conv[..., 2 * H_A * DK:].reshape(bsz, t_len, H_A, DV)
    beta = jax.nn.sigmoid(b_in.astype(jnp.float32))
    g = -jnp.exp(a_log.astype(jnp.float32)) * jax.nn.softplus(
        a_in.astype(jnp.float32) + dt_bias.astype(jnp.float32))
    o, s_new = _gated_delta_chunked(q, k, v, g, beta, s0)
    o = _rms_norm(o.astype(h.dtype), o_norm) * jax.nn.silu(gate.reshape(bsz, t_len, H_A, DV))
    return o.reshape(bsz, t_len, H_A * DV) @ w_out, new_conv, s_new.astype(h.dtype)

def _stick_breaking(q, k, v, bias, q_start):
    f32 = jnp.float32
    t_q = q.shape[1]
    qb = min(Q_BLOCK, t_q)
    scale = HD_B ** -0.5
    bias_f = bias.astype(f32)[None, :, None, None]
    outs = []
    for s0 in range(0, t_q, qb):
        s1 = min(s0 + qb, t_q)
        n_keys = q_start + s1
        kb, vb = k[:, :n_keys], v[:, :n_keys]
        z = jnp.einsum('bqhd,bkhd->bhqk', q[:, s0:s1].astype(f32), kb.astype(f32)) * scale + bias_f
        q_pos = q_start + s0 + jnp.arange(s1 - s0)
        k_pos = jnp.arange(n_keys)
        mask = k_pos[None, :] < q_pos[:, None]
        log_keep = jnp.where(mask, jax.nn.log_sigmoid(-z), 0.0)
        after = lax.cumsum(log_keep, axis=3, reverse=True) - log_keep
        att = jnp.where(mask, jnp.exp(jax.nn.log_sigmoid(z) + after), 0.0)
        outs.append(jnp.einsum('bhqk,bkhd->bqhd', att.astype(v.dtype), vb))
    return jnp.concatenate(outs, axis=1)

def _sb_mixer(h, k_all, v_all, q_start, w_q, bias, w_o):
    bsz, t_len, _ = h.shape
    q = (h @ w_q).reshape(bsz, t_len, H_B, HD_B)
    o = _stick_breaking(q, k_all, v_all, bias, q_start)
    return o.reshape(bsz, t_len, H_B * HD_B) @ w_o

def _trunk(x, p, conv0, rec0, k_past, v_past, w):
    bsz, t_len, _ = x.shape
    q_start = 0 if k_past is None else k_past.shape[1]
    convs, recs = [], []
    k_all = v_all = k_new = v_new = None
    for i in range(DEPTH):
        x = x + 0.5 * _swiglu(_rms_norm(x, w['ffn1_norm'][i]), w['ffn1_w_in'][i], w['ffn1_w_out'][i])
        h = _rms_norm(x, w['mix_norm'][i])
        if i < N_A:
            y, c_new, s_new = _gdn_mixer(h, conv0[i], rec0[i], w['a_w_in'][i], w['a_conv'][i],
                                         w['a_A_log'][i], w['a_dt_bias'][i], w['a_o_norm'][i],
                                         w['a_w_out'][i])
            convs.append(c_new)
            recs.append(s_new)
        else:
            y = _sb_mixer(h, k_all, v_all, q_start, w['b_w_q'][i - N_A], w['b_bias'][i - N_A],
                          w['b_w_o'][i - N_A])
        x = x + y
        x = x + 0.5 * _swiglu(_rms_norm(x, w['ffn2_norm'][i]), w['ffn2_w_in'][i], w['ffn2_w_out'][i])
        x = x + (p[i] @ w['ple_w_in'][i]) * jax.nn.sigmoid(
            _rms_norm(x, w['ple_norm'][i]) @ w['ple_w_gate'][i])
        if i == N_A - 1:
            kv = _rms_norm(x, w['kv_norm']) @ w['w_kv']
            k_new = kv[..., :H_B * HD_B].reshape(bsz, t_len, H_B, HD_B)
            v_new = kv[..., H_B * HD_B:].reshape(bsz, t_len, H_B, HD_B)
            if k_past is None:
                k_all, v_all = k_new, v_new
            else:
                k_all = jnp.concatenate([k_past.astype(k_new.dtype), k_new], axis=1)
                v_all = jnp.concatenate([v_past.astype(v_new.dtype), v_new], axis=1)
    y = _rms_norm(x, w['final_norm'])
    return y, jnp.stack(convs), jnp.stack(recs), k_new, v_new

def setup_inputs(seed: int = 0) -> dict:
    key = jax.random.key(seed)
    keys = iter(jax.random.split(key, 48))
    f32 = jnp.float32

    def nrm(shape, scale=1.0):
        return jax.random.normal(next(keys), shape, f32) * scale

    def gain(shape):
        return 1.0 + 0.02 * jax.random.normal(next(keys), shape, f32)

    n_pages = PAST_LEN // PAGE_SIZE
    n_used = DEC_BATCH * n_pages
    n_phys = n_used + max(1, n_used // 4)
    page_table = jax.random.permutation(next(keys), n_phys)[:n_used].reshape(
        DEC_BATCH, n_pages).astype(jnp.int32)
    dt = jax.random.uniform(next(keys), (N_A, H_A), f32, minval=0.001, maxval=0.1)
    return {
        'x_prompt': nrm((BATCH, SEQ, D_MODEL)),
        'x_sample': nrm((DEC_BATCH, DEC_SEQ, D_MODEL)),
        'cache_k': nrm((n_phys, PAGE_SIZE, H_B, HD_B)),
        'cache_v': nrm((n_phys, PAGE_SIZE, H_B, HD_B)),
        'state_conv': nrm((N_A, DEC_BATCH, CONV_W - 1, QKV_DIM)),
        'state_rec': nrm((N_A, DEC_BATCH, H_A, DK, DV), 0.1),
        'page_table': page_table,
        'p_prompt': nrm((DEPTH, BATCH, SEQ, P_DIM)),
        'p_sample': nrm((DEPTH, DEC_BATCH, DEC_SEQ, P_DIM)),
        'ffn1_norm': gain((DEPTH, D_MODEL)),
        'ffn1_w_in': nrm((DEPTH, D_MODEL, 2 * D_FF), D_MODEL ** -0.5),
        'ffn1_w_out': nrm((DEPTH, D_FF, D_MODEL), D_FF ** -0.5),
        'mix_norm': gain((DEPTH, D_MODEL)),
        'ffn2_norm': gain((DEPTH, D_MODEL)),
        'ffn2_w_in': nrm((DEPTH, D_MODEL, 2 * D_FF), D_MODEL ** -0.5),
        'ffn2_w_out': nrm((DEPTH, D_FF, D_MODEL), D_FF ** -0.5),
        'ple_w_in': nrm((DEPTH, P_DIM, D_MODEL), P_DIM ** -0.5),
        'ple_norm': gain((DEPTH, D_MODEL)),
        'ple_w_gate': nrm((DEPTH, D_MODEL, D_MODEL), D_MODEL ** -0.5),
        'a_w_in': nrm((N_A, D_MODEL, PROJ_A), D_MODEL ** -0.5),
        'a_conv': nrm((N_A, CONV_W, QKV_DIM), CONV_W ** -0.5),
        'a_A_log': jnp.log(jax.random.uniform(next(keys), (N_A, H_A), f32, minval=1.0, maxval=16.0)),
        'a_dt_bias': dt + jnp.log(-jnp.expm1(-dt)),
        'a_o_norm': gain((N_A, DV)),
        'a_w_out': nrm((N_A, H_A * DV, D_MODEL), (H_A * DV) ** -0.5),
        'kv_norm': gain((D_MODEL,)),
        'w_kv': nrm((D_MODEL, 2 * H_B * HD_B), D_MODEL ** -0.5),
        'b_w_q': nrm((N_B, D_MODEL, H_B * HD_B), D_MODEL ** -0.5),
        'b_bias': SB_BIAS_INIT + 0.5 * jax.random.normal(next(keys), (N_B, H_B), f32),
        'b_w_o': nrm((N_B, H_B * HD_B, D_MODEL), (H_B * HD_B) ** -0.5),
        'final_norm': gain((D_MODEL,)),
    }

def reference(x_prompt, x_sample, cache_k, cache_v, state_conv, state_rec, page_table,
              p_prompt, p_sample, ffn1_norm, ffn1_w_in, ffn1_w_out, mix_norm, ffn2_norm,
              ffn2_w_in, ffn2_w_out, ple_w_in, ple_norm, ple_w_gate, a_w_in, a_conv, a_A_log,
              a_dt_bias, a_o_norm, a_w_out, kv_norm, w_kv, b_w_q, b_bias, b_w_o, final_norm):
    w = dict(ffn1_norm=ffn1_norm, ffn1_w_in=ffn1_w_in, ffn1_w_out=ffn1_w_out,
             mix_norm=mix_norm, ffn2_norm=ffn2_norm, ffn2_w_in=ffn2_w_in,
             ffn2_w_out=ffn2_w_out, ple_w_in=ple_w_in, ple_norm=ple_norm,
             ple_w_gate=ple_w_gate, a_w_in=a_w_in, a_conv=a_conv, a_A_log=a_A_log,
             a_dt_bias=a_dt_bias, a_o_norm=a_o_norm, a_w_out=a_w_out, kv_norm=kv_norm,
             w_kv=w_kv, b_w_q=b_w_q, b_bias=b_bias, b_w_o=b_w_o, final_norm=final_norm)

    bp = x_prompt.shape[0]
    conv0_p = [jnp.zeros((bp, CONV_W - 1, QKV_DIM), x_prompt.dtype) for _ in range(N_A)]
    rec0_p = [jnp.zeros((bp, H_A, DK, DV), x_prompt.dtype) for _ in range(N_A)]
    y_prompt, conv_prompt, rec_prompt, k_prompt, v_prompt = _trunk(
        x_prompt, p_prompt, conv0_p, rec0_p, None, None, w)

    db, n_pages = page_table.shape
    k_past = cache_k[page_table].reshape(db, n_pages * cache_k.shape[1], H_B, HD_B)
    v_past = cache_v[page_table].reshape(db, n_pages * cache_v.shape[1], H_B, HD_B)
    conv0_s = [state_conv[i] for i in range(N_A)]
    rec0_s = [state_rec[i] for i in range(N_A)]
    y_sample, conv_sample, rec_sample, k_sample, v_sample = _trunk(
        x_sample, p_sample, conv0_s, rec0_s, k_past, v_past, w)

    return (y_prompt, y_sample, conv_prompt, rec_prompt, k_prompt, v_prompt,
            conv_sample, rec_sample, k_sample, v_sample)


_drawn_inputs = setup_inputs


def setup_inputs(seed=0):
    import zlib

    import numpy as np

    out = dict(_drawn_inputs(seed))
    spreads = {}
    factors = {'cache_k': 6.458,
     'cache_v': 5.067,
     'ffn1_norm': 4.573,
     'ffn2_norm': 6.459,
     'ple_norm': 200.0,
     'a_o_norm': 5.499,
     'kv_norm': 7.838,
     'b_w_q': 5.923,
     'b_bias': 8.0,
     'b_w_o': 3.625,
     'final_norm': 21.015}
    for name, (base, spread) in spreads.items():
        noise = np.random.default_rng([zlib.crc32(name.encode()), seed]).standard_normal(out[name].shape)
        drawn = base * np.exp(spread * noise) if base else spread * noise
        out[name] = __import__('jax').numpy.asarray(drawn.astype(out[name].dtype))
    for name, factor in factors.items():
        out[name] = (out[name] * factor).astype(out[name].dtype)
    return out
```

```python
from contextlib import ExitStack

import concourse.bass as bass
from concourse import mybir

F32 = mybir.dt.float32
F32R = mybir.dt.float32r
I32 = mybir.dt.int32
ALU = mybir.AluOpType
ACT = mybir.ActivationFunctionType
ds = bass.ds

P = 128
NEG_BIG = -1.0e30
SOFTPLUS_CAP = 40.0
EPS = 1e-6
SLOT = 2048


class Step:

    def __init__(self, kind, stats=False, after=None, sums=False, fills=(), layer=0, units=0, ka=0, kb=0, loads=None,
                 view=None, rhs=None, dst=None, scale=1.0, coef=1.0):
        self.kind = kind
        self.stats = stats
        self.after = after
        self.sums = sums
        self.fills = fills
        self.layer = layer
        self.units = units
        self.ka, self.kb = ka, kb
        self.loads, self.view, self.rhs = loads, view, rhs
        self.dst, self.scale, self.coef = dst, scale, coef
        self.n = {}


def program(nc, A, O):
    _, TP, D = A["x_prompt"].shape
    NB, TD, _ = A["x_sample"].shape
    TS = NB * TD
    T = TP + TS
    HC = T // 2
    KD = D // P
    FF = A["ffn1_w_in"].shape[2] // 2
    FT = FF // P
    PK = A["p_prompt"].shape[-1] // P
    QKV = A["a_conv"].shape[-1]
    CT = QKV // P
    HA = A["a_A_log"].shape[-1]
    CW = A["a_conv"].shape[1]
    CP = CW - 1
    DH = P
    PROJ = A["a_w_in"].shape[-1]
    HB = A["b_bias"].shape[-1]
    HD = D // HB
    PT = TP // P
    NT = PT + 1
    NPG = A["page_table"].shape[1]
    NPHYS, PGS = A["cache_k"].shape[:2]
    assert (T, HC, KD, HA, CW, PK, NPG, HD, PGS, TS) == (576, 288, 8, 8, 4, 2, 2, 64, 128, 64) and CT == 3 * HA
    XP = CP + TP + NB * (CP + TD)
    XC = XP - CP
    GROUPS = [(0, KD), (KD, KD), (2 * KD, FT - 2 * KD)]
    AB0 = PROJ - P
    RB = 96
    NR = P - RB
    RA = NR - 2 * HA

    ctx = ExitStack()
    with ctx:
        base = (nc.sbuf_base + 31) // 32 * 32
        room = (nc.sbuf_usable_end - 64 - base) // 32 * 32

        def size(shape):
            n = 4
            for s in shape[1:]:
                n *= s
            return (n + 31) // 32 * 32

        class Region:

            def __init__(self, start, end):
                self.at, self.end = start, end

            def take(self, name, shape, dt=F32):
                t = nc.alloc_sbuf_tensor_at(name, shape, dt, offset=base + self.at)
                self.at += size(shape)
                assert self.at <= self.end, (name, self.at, self.end)
                return t

        def sem(name):
            return ctx.enter_context(nc.semaphore(name))

        whole = Region(0, room)
        xT = whole.take("xT", [P, KD, T])
        w_hi = whole.take("w_hi", [P, 2, KD, P], F32R)
        w_lo = whole.take("w_lo", [P, 2, KD, P], F32R)
        raw = whole.take("raw", [P, 2, SLOT])
        p_hi = whole.take("p_hi", [P, PK, T], F32R)
        p_lo = whole.take("p_lo", [P, PK, T], F32R)
        norm0 = whole.at
        rs = whole.take("rs", [P, T])
        ssum = whole.take("ssum", [P, T])
        std = whole.take("std", [P, T])
        norm1 = whole.at
        ident = whole.take("ident", [P, P])
        ones = whole.take("ones", [P, P])
        triu = whole.take("triu", [P, P])
        tril = whole.take("tril", [P, P])
        lt = whole.take("lt", [P, P])
        neg_lt = whole.take("neg_lt", [P, P])
        same = whole.take("same", [TS, TS])
        triu_s = whole.take("triu_s", [TS, TS])
        lt_s = whole.take("lt_s", [TS, TS])
        neg_lt_s = whole.take("neg_lt_s", [TS, TS])
        eps = whole.take("eps", [P, 1])
        gain = whole.take("gain", [P, 10 * KD + 1])
        bias_b = whole.take("bias_b", [P, HB])
        pages = whole.take("pages", [1, NB * NPG], I32)
        bias_c = whole.take("bias_c", [P, 2, 2])
        scratch0 = whole.at
        gate_s = whole.take("gate_s", [P, T])
        up_s = whole.take("up_s", [P, T])
        gate_f = whole.take("gate_f", [P, T])
        hid_f = whole.take("hid_f", [P, T])
        sqb = whole.take("sqb", [P, 2, T])
        hx0 = whole.at
        hx_hi = whole.take("hx_hi", [P, KD, T], F32R)
        hx_lo = whole.take("hx_lo", [P, KD, T], F32R)
        hx1 = whole.at
        hid_hi = whole.take("hid_hi", [P, KD, T], F32R)
        hid_lo = whole.take("hid_lo", [P, KD, T], F32R)
        tail0 = whole.at

        r = Region(hx1, tail0)
        x_rows = r.take("x_rows", [P, NT, D])
        gain_rows = r.take("gain_rows", [10 * KD + 1, P])
        conv_rows = r.take("conv_rows", [CW * CT, P])
        old_rows = r.take("old_rows", [NB * CP, QKV])
        r = Region(hx1, room)
        qkv = r.take("qkv", [P, CT, T])
        gates = r.take("gates", [P, HA, T])
        small0 = r.at
        lm = r.take("lm", [P, 7, P])
        conv_w = r.take("conv_w", [P, CW, CT])
        neg_le = r.take("neg_le", [P, P])
        neg_le_s = r.take("neg_le_s", [TS, TS])
        a_col = r.take("a_col", [P, 1])
        ea_col = r.take("ea_col", [P, 1])
        dt_col = r.take("dt_col", [P, 1])
        e32 = r.take("e32", [P, 32])
        hot = r.take("hot", [P, 31])
        small1 = r.at
        xpad = r.take("xpad", [P, 2, XP])
        old_T = r.take("old_T", [P, CT, NB * CP])
        r = Region(scratch0, hx0)
        cv = r.take("cv", [P, 2, XP])
        new_T = r.take("new_T", [P, CT, CP + NB * CP])
        r = Region(hx0, hx1)
        new_rows = r.take("new_rows", [CP + NB * CP, QKV])
        r = Region(tail0, room)
        kT = r.take("kT", [P, KD, T])
        v_tok = r.take("v_tok", [P, NT, D])
        tail1 = r.at
        p_f, p_rows = [], []
        for layer, r in enumerate((Region(tail0, small0), Region(tail1, room))):
            p_f.append(r.take(f"p_f{layer}", [P, PK, T]))
            p_rows.append(r.take(f"p_rows{layer}", [P, NT, PK * P]))
        vT = Region(hx1, tail0).take("vT", [P, KD, T])
        tok_out = Region(scratch0, hx0).take("tok_out", [P, 2, D])
        r = Region(hx0, tail0)
        yT = r.take("yT", [P, KD, T])
        r = Region(hx1, tail0)
        qT = r.take("qT", [P, KD, T])
        r = Region(small1, room)
        ab = r.take("ab", [P, T])

        ps = ctx.enter_context(nc.psum_tensor("ps", [P, 8, 512], F32))
        TILE = (ps[:, 0:2, 0:HC], ps[:, 2:4, 0:HC])
        STAT = ps[:, 4:6, 0:HC]

        def halves(ap):
            return ap.rearrange("p (c n) -> p c n", c=2)

        def seqs(ap, n=TD):
            return ap.rearrange("p (b t) -> p b t", t=n)

        raw_in = [sem("raw_in0"), sem("raw_in1")]
        w_hi_done = sem("w_hi_done")
        w_lo_done = sem("w_lo_done")
        tile_done = sem("tile_done")
        evac = [sem("evac_a"), sem("evac_b")]
        silu_done = sem("silu_done")
        hid_mul = sem("hid_mul")
        hid_hi_done = sem("hid_hi_done")
        hid_done = sem("hid_done")
        hx_hi_done = sem("hx_hi_done")
        hx_done = sem("hx_done")
        x_add = sem("x_add")
        sq_done = sem("sq_done")
        ssum_zero = sem("ssum_zero")
        ssum_done = sem("ssum_done")
        stat_done = sem("stat_done")
        std_done = sem("std_done")
        rs_done = sem("rs_done")
        const_zero = sem("const_zero")
        const_done = sem("const_done")
        x_in = sem("x_in")
        gain_in = sem("gain_in")
        small_in = sem("small_in")
        col_in = sem("col_in")
        old_in = sem("old_in")
        p_in = sem("p_in")
        setup_tr = sem("setup_tr")
        setup_ev = sem("setup_ev")
        p_tr = sem("p_tr")
        p_ev = sem("p_ev")
        p_hi_done = sem("p_hi_done")
        p_done = sem("p_done")
        y_done = sem("y_done")
        stored = sem("stored")
        pad_ready = sem("pad_ready")
        tap_done = sem("tap_done")
        conv_step = sem("conv_step")
        conv_done = sem("conv_done")
        new_done = sem("new_done")
        newt_tr = sem("newt_tr")
        newt_ev = sem("newt_ev")
        tok_tr = sem("tok_tr")
        tok_ev = [sem("tok_ev_vector"), sem("tok_ev_scalar")]
        tok_stored = [sem("tok_stored0"), sem("tok_stored1")]

        def pair_loads(w, col0, k0=0, k=KD):
            wv = w.rearrange("(k p) n -> p k n", p=P)
            half = k // 2

            def view(slot):
                return slot[:, 0:k * 2 * P].rearrange("p (k n) -> p k n", n=2 * P)

            def loads(u, slot):
                cols = ds(u * (2 * P) + col0, 2 * P)
                return [(view(slot)[:, a:b], wv[:, k0 + a:k0 + b, cols]) for a, b in ((0, half), (half, k))]
            return loads, lambda m, slot: view(slot)[:, :, m * P:(m + 1) * P]

        def two_loads(wa, ca, wb, cb, ka, kb):
            va, vb = (w.rearrange("(k p) n -> p k n", p=P) for w in (wa, wb))

            def view(m, slot):
                k = (ka, kb)[m]
                return slot[:, m * KD * P:m * KD * P + k * P].rearrange("p (k n) -> p k n", n=P)

            def loads(u, slot):
                return [(view(0, slot), va[:, 0:ka, ds(u * P + ca, P)]),
                        (view(1, slot), vb[:, 0:kb, ds(u * P + cb, P)])]
            return loads, view

        SETUP_FILLS = 13
        plan = []
        HX, HID, PR = (hx_hi, hx_lo), (hid_hi, hid_lo), (p_hi, p_lo)
        FFN1, MIX, FFN2, PLE, KVN, FIN, ON = (n * KD for n in (0, 2, 4, 6, 8, 9, 10))

        def stage(kind, **more):
            plan.append(Step(kind, **more))

        def product(kind, units, ka, kb, lv, rhs, **more):
            stage(kind, units=units, ka=ka, kb=kb, loads=lv[0], view=lv[1], rhs=rhs, **more)

        def ffn(name, layer, after, stats=True):
            w_in, w_out = A[name + "_w_in"][layer], A[name + "_w_out"][layer]
            for n, (f0, k) in enumerate(GROUPS):
                product("gu", k, KD, KD, two_loads(w_in, f0 * P, w_in, FF + f0 * P, KD, KD), HX, stats=stats and n == 0)
                last = n == len(GROUPS) - 1
                product("upd", KD // 2, k, k, pair_loads(w_out, 0, f0, k), HID, coef=0.5,
                        after=after if last else None, sums=last)

        def ple(layer, after):
            product("ple", KD, KD, PK, two_loads(A["ple_w_gate"][layer], 0, A["ple_w_in"][layer], 0, KD, PK),
                    HX, stats=True, after=after, sums=True)

        def rows_of(src, dst):
            out = []
            for i in range(NT):
                n = P if i < PT else TS
                for half in range(2):
                    to = (tok_out[0:n, i % 2] if dst is None else dst[0:n, i])[:, half * D // 2:(half + 1) * D // 2]
                    out.append(([src[:, KD // 2 * half + q, i * P:i * P + n] for q in range(KD // 2)], to, i))
            return out

        stage("setup", after=FFN1, sums=True)
        stage("p", layer=0)
        ffn("ffn1", 0, MIX)
        w_a = A["a_w_in"][0]
        product("qkv", CT // 2, KD, KD, pair_loads(w_a, 0), HX, stats=True)
        product("gate", HA // 2, KD, KD, pair_loads(w_a, QKV), HX)
        product("ab", 1, KD, 1, two_loads(w_a, AB0, w_a, AB0, KD, 1), HX)
        stage("newrows", fills=[([new_T[:, 4 * g + q] for q in range(4)], new_rows[:, 4 * g * P:4 * (g + 1) * P], 0)
                                for g in range(CT // 4)])
        stage("gdn")
        product("upd", KD // 2, KD, KD, pair_loads(A["a_w_out"][0], 0), HID, coef=1.0, after=FFN2 + 0, sums=True)
        ffn("ffn2", 0, PLE)
        ple(0, None)
        stage("regain", after=KVN)
        product("lin", KD // 2, KD, KD, pair_loads(A["w_kv"], 0), HX, stats=True, dst=kT, scale=1.0)
        product("lin", KD // 2, KD, KD, pair_loads(A["w_kv"], D), HX, dst=vT, scale=1.0)
        stage("kvout", after=FFN1 + KD, fills=rows_of(kT, None) + rows_of(vT, v_tok))
        stage("p", layer=1)
        ffn("ffn1", 1, MIX + KD, stats=False)
        product("lin", KD // 2, KD, KD, pair_loads(A["b_w_q"][0], 0), HX, stats=True, dst=qT, scale=HD ** -0.5)
        stage("attend")
        product("upd", KD // 2, KD, KD, pair_loads(A["b_w_o"][0], 0), HID, coef=1.0, after=FFN2 + KD, sums=True)
        ffn("ffn2", 1, PLE + KD)
        ple(1, None)
        stage("final", fills=rows_of(yT, None))

        count = dict.fromkeys(("unit", "eb", "gu", "hid", "hx", "sum", "stat", "ple", "gs", "tok"), 0)
        for s in plan:
            s.n = dict(count)
            count["unit"] += s.units
            count["eb"] += s.units if s.kind != "ab" else 0
            count["tok"] += len(s.fills)
            count["stat"] += s.stats or s.kind == "final"
            count["sum"] += s.sums
            count["hx"] += s.after is not None
            if s.kind == "gu":
                count["gu"] += s.units
                count["hid"] += s.units
            if s.kind in ("gu", "ple", "gate"):
                count["gs"] += s.units * (2 if s.kind == "gate" else 1)
            if s.kind == "ple":
                count["ple"] += 1
            if s.kind in ("gdn", "attend"):
                count["hid"] += KD
        products = [s for s in plan if s.units]
        following = {id(s): f for s, f in zip(products, products[1:] + [None])}

        def in_pairs(eng, s, body):
            loop = (s.units - 1) // 2
            start = 1 if s.stats and loop else 0
            if loop - start < 2:
                start = loop
            for i in range(start):
                body(i, 0, (s, i, 1))
                body(i, 1, (s, i + 1, 0))
            if start < loop:
                with eng.Fori(start, loop) as i:
                    body(i, 0, (s, i, 1))
                    body(i, 1, (s, i + 1, 0))
            if s.units % 2 == 0:
                body(loop, 0, (s, loop, 1))
                body(loop, 1, (following[id(s)], 0, 0))
            else:
                body(loop, 0, (following[id(s)], 0, 0))

        def unit_no(s, i, r):
            return i * 2 + (s.n["unit"] + r)

        def slot_of(s, r):
            return raw[:, (s.n["unit"] + r) % 2, :], raw_in[(s.n["unit"] + r) % 2]

        def split_hi(act, target, m):
            s, i, r = target
            if s is None:
                return
            slot, landed = slot_of(s, r)
            k = (s.ka, s.kb)[m]
            act.wait_ge(landed, i * 32 + 32 * ((s.n["unit"] + r) // 2 + 1))
            if not (isinstance(i, int) and unit_no(s, i, r) == 0):
                act.wait_ge(tile_done, unit_no(s, i, r) * 2 + (m - 1))
            nc.scalar.activation(w_hi[:, m, 0:k], s.view(m, slot), ACT.Copy).then_inc(w_hi_done, 1)

        def split_lo(dve, target, m):
            s, i, r = target
            if s is None:
                return
            slot, _ = slot_of(s, r)
            k = (s.ka, s.kb)[m]
            dve.wait_ge(w_hi_done, unit_no(s, i, r) * 2 + (m + 1))
            nc.vector.tensor_tensor(w_lo[:, m, 0:k], s.view(m, slot), w_hi[:, m, 0:k].bitcast(F32),
                                    ALU.subtract).then_inc(w_lo_done, 1)

        def multiply(pe, s, u, m):
            k_all = (s.ka, s.kb)[m]
            hi, lo = (PR if s.kind == "ple" and m == 1 else s.rhs)
            n = s.n["unit"]
            pe.wait_ge(w_lo_done, u * 2 + (2 * n + m + 1))
            if isinstance(u, int) and n + u == 0:
                pe.wait_ge(setup_ev, SETUP_FILLS)
            else:
                pe.wait_ge(evac[m], u + (n, s.n["eb"])[m])
            for k in range(k_all):
                if hi is hx_hi:
                    pe.wait_ge(hx_done, KD * (s.n["hx"] - 1) + k + 1)
                elif hi is hid_hi:
                    pe.wait_ge(hid_done, s.n["hid"] - k_all + k + 1)
                else:
                    pe.wait_ge(p_done, PK * (s.n["ple"] + 1))
                for a, (w, h) in enumerate(((w_hi, hi), (w_hi, lo), (w_lo, hi))):
                    for c in range(2):
                        last = nc.tensor.matmul(TILE[m][:, c], w[:, m, k], h[:, k, c * HC:(c + 1) * HC],
                                                start=k == 0 and a == 0, stop=k == k_all - 1 and a == 2)
            last.then_inc(tile_done, 1)

        def pe_stats(pe, s, r):
            pe.wait_ge(ssum_done, KD * (r + 1))
            if r:
                pe.wait_ge(std_done, r)
                pe.wait_ge(rs_done, r)
            for par in range(2):
                if (s.n["tok"] + 1 - par) // 2:
                    pe.wait_ge(tok_ev[par], (s.n["tok"] + 1 - par) // 2)
            pe.wait_ge(p_ev, 3 * (s.n["ple"] + (s.kind != "final" and not (s.kind == "lin" and s.dst is kT))))
            for c in range(2):
                last = nc.tensor.matmul(STAT[:, c], ones[:], ssum[:, c * HC:(c + 1) * HC], start=True, stop=True)
            last.then_inc(stat_done, 1)

        def act_stats(act, r):
            act.wait_ge(stat_done, r + 1)
            if r:
                act.wait_ge(rs_done, r)
            nc.scalar.activation(halves(std[:]), STAT, ACT.Sqrt, bias=eps[:], scale=1.0 / D).then_inc(std_done, 1)

        def dve_stats(dve, r):
            dve.wait_ge(std_done, r + 1)
            nc.vector.reciprocal(rs[:], std[:]).then_inc(rs_done, 1)

        LEVELS = 7
        S_LEVELS = 3
        order = {}

        def steps(owner, names):
            s = sem(owner)
            for n, name in enumerate(names.split()):
                assert name not in order, name
                order[name] = (s, n + 1)

        said = {}

        def done(name, ins):
            s, n = order[name]
            said[id(s)] = said.get(id(s), 0) + 1
            assert said[id(s)] == n, name
            ins.then_inc(s, 1)

        def after(eng, *names):
            for name in names:
                eng.wait_ge(*order[name])

        steps("gdn_tensor", "tok_ab gc_all bc_s kk_s qk_s vt_s kt_s xtr_s am1_s dm1_s dtm1_s am2_s dtm2_s wm_s ut_s "
                            "sw_s vtr_s om_s " + " ".join(f"su{h}_s" for h in range(HA)))
        steps("gdn_vector", "z sp g tokc0 tokc1 rec rows_gc rows_gcs rows_be rows_bes cst0 cst1 kdx0 kdx1 be0 be1 "
                            "mq_s mk_s mg_s mb_s qn_s kn_s kb_s qd_s dsub_s dneg_s mt_s qkm_s vb_s kbg_s kd_s gts_s "
                            "mo0_s xt0_s mo1_s xu1_s xtu1_s mo2_s xtu2_s vnt_s os_s vnc_s osum_s "
                            + "vnm0_s " + " ".join(f"vnm{h}_s upd{h - 1}_s" for h in range(1, HA)) + f" upd{HA - 1}_s orec")
        steps("gdn_scalar", "ea e l sg std16 ex0 ex1 exk0 exk1 eb_s dexp_s xc_s acp1_s acp2_s wn_s utc_s ostd")
        steps("gdn_pool", " ".join(f"stg{h}_s" for h in range(HA)))
        g = {n: sem("gdn_" + n) for n in (
            "square", "summed", "sel", "bc", "qn", "kn", "kb", "dsub", "eb", "dexp", "qd", "vcopy", "kk", "qk", "vt", "kt",
            "mt", "qkm", "vb", "kbg", "kd", "mo", "xtr", "xc", "am", "acp", "dm", "dtm", "xu", "xtu", "wm", "wn",
            "vm", "vcp", "om", "ocp", "sm", "su", "osq", "osum", "mask", "bco", "of", "og")}
        s_out = sem("s_out")
        st_in = sem("st_in")
        qs_out = sem("st_out")

        r = Region(small1, room)
        r.take("ab_again", [P, T])
        rows = r.take("rows", [P, T])
        over_sg = Region(r.at, r.at + size([P, T]))
        sg = r.take("sg", [P, T])
        tokc = r.take("tokc", [P, NT, 2 * NR])
        sel = r.take("sel", [P, 2, 2, P])
        cst = r.take("cst", [P, 2 * PT * HA + 2 * HA])
        est = r.take("est", [P, 2 * PT * HA + 2 * HA])
        bec = r.take("bec", [P, NT * HA])
        kdc = r.take("kdc", [P, NT * HA])
        state = over_sg.take("state", [P, 2, DH])
        gts = over_sg.take("gts", [P, HA * NB])
        C_G, C_B = RA, NR + RA + HA
        C_E, C_S = PT * HA, 2 * PT * HA

        r = Region(scratch0, hx1)
        z_buf, e_buf, l_buf, std16 = (r.take(n, [P, T]) for n in ("z_buf", "e_buf", "l_buf", "std16"))
        sqk = r.take("sqk", [P, 2, T])
        r = Region(scratch0, hx1)
        names = ("knT", "kbT", "qnT", "qdT", "dx", "mt", "x", "xt", "vb", "kbg", "kd", "qkm")
        lane = [{n: r.take(f"{n}{a}", [P, PT, P]) for n in names} for a in range(2)]
        for a in range(2):
            lane[a]["vn"] = r.take(f"vn{a}", [P, P])
            lane[a]["A"], lane[a]["mo"], lane[a]["wn"], lane[a]["eb"], lane[a]["vc"] = (
                lane[a][n] for n in ("kbT", "dx", "x", "mt", "x"))
        r = Region(scratch0, hx1)
        vnm = [r.at]
        kn_s, kb_s = r.take("kn_s", [P, HA, TS]), r.take("kb_s", [P, HA, TS])
        vnm.append(r.at)
        qn_s, eb_s = r.take("qn_s", [P, HA, TS]), r.take("eb_s", [P, HA, TS])
        vnm = [Region(v, r.at).take(f"vnm{n}", [TS, NB, DH]) for n, v in enumerate(vnm)]
        wq_s = r.take("wq_s", [P, HA * NB, 2 * TD])
        dx_s, mt_s, x_s, xt_s, qkm_s = (r.take(n, [P, HA, TS]) for n in ("dx_s", "mt_s", "x_s", "xt_s", "qkm_s"))
        vb_s, kbg_s, kd_s = (r.take(n, [TS, HA, DH]) for n in ("vb_s", "kbg_s", "kd_s"))
        vnT_s, oT_s = (r.take(n, [P, HA, TS]) for n in ("vnT_s", "oT_s"))
        A_s, mo_s, vn_s = eb_s, dx_s, kbg_s
        r = Region(scratch0, hx0)
        osq = r.take("osq", [P, 2, T])
        omask = r.take("omask", [P, 2, T])
        ostd = r.take("ostd", [P, T])
        r = Region(hx1 + 2 * HA * size([P, T]), small0)
        of = r.take("of", [P, 2, T])
        og = r.take("og", [P, 2, T])

        def st(h):
            return qkv[:, HA + 2 * h:HA + 2 * h + 2, 0:TP].rearrange("p c (b d) -> p c b d", d=DH)

        def st1(h, b):
            return qkv[:, HA + 2 * h + b // PT, (b % PT) * DH:(b % PT + 1) * DH]

        def bank(n, k=1):
            return ps[:, n] if k == 1 else ps[:, n:n + k].rearrange("p b n -> p (b n)")

        def by_head(ap):
            return ap.rearrange("p (h t) -> p h t", h=HA)

        def cnt(hp, a, per_head, n):
            return hp * (2 * per_head) + (2 * n + a + 1)

        def dyn(ap, at):
            return ap[:, ds(at, 1)].squeeze(1)

        def gdn_sp(sp, s):
            with sp.Fori(0, HA // 2) as hp:
                for a in range(2):
                    sp.wait_ge(g["su"], cnt(hp, a, PT, PT - 1))
                    sp.dma_start(O["rec_prompt"][0, 0][ds(hp * 2 + a, 1)].squeeze(0), state[:, a]).then_inc(s_out, 16)
            sp.wait_ge(g["vt"], HA)
            sp.wait_ge(g["kn"], HA)
            for h in range(HA):
                src = A["state_rec"][0].rearrange("b h k v -> h k b v")[h]
                for c in range(2):
                    sp.dma_start(st(h)[:, c], src[:, c * PT:(c + 1) * PT]).then_inc(st_in, 16)
            for h in range(HA):
                after(sp, f"upd{h}_s")
                dst = O["rec_sample"][0].rearrange("b h k v -> h k b v")[h]
                for c in range(2):
                    sp.dma_start(dst[:, c * PT:(c + 1) * PT], st(h)[:, c]).then_inc(qs_out, 16)

        def gdn_pool(pool, s):
            def mask(hp, a, level):
                L = lane[a]
                if level == 0:
                    pool.wait_ge(g["mt"], hp * 2 + (a + 1))
                    pool.wait_ge(g["qkm"], hp * 2 + (a + 1))
                elif level == 1:
                    pool.wait_ge(g["xtu"], cnt(hp, a, LEVELS, 0))
                else:
                    pool.wait_ge(g["am"], cnt(hp, a, LEVELS - 1, level - 2))
                nc.gpsimd.tensor_tensor(L["mo"][:], L["mt"][:], lm[:, level].unsqueeze(1).to_broadcast((P, PT, P)),
                                        ALU.mult).then_inc(g["mo"], 1)

            pool.wait_ge(tile_done, 2 * s.n["unit"])
            with pool.Fori(0, HA // 2) as hp:
                for a in range(2):
                    for n in range(2):
                        nc.gpsimd.tensor_copy(sel[:, a, n], e32[:, ds(hp * 2 + (a + n * HA), 1)].to_broadcast((P, P))
                                              ).then_inc(g["sel"], 1)
                for level in range(LEVELS):
                    for a in range(2):
                        mask(hp, a, level)
            for h in range(HA):
                pool.wait_ge(st_in, 32 * HA)
                after(pool, "sw_s", "gts_s")
                gt = gts[:, h * NB:(h + 1) * NB].rearrange("p (c b) -> p c b", c=2).unsqueeze(3).to_broadcast((P, 2, PT, DH))
                done(f"stg{h}_s", nc.gpsimd.tensor_tensor(st(h), st(h), gt, ALU.mult))
            with pool.Fori(0, HA // 2) as hp:
                for a in range(2):
                    pool.wait_ge(g["of"], hp * 2 + (a + 1))
                    nc.gpsimd.tensor_tensor(og[:, a], of[:, a], dyn(gates, hp * 2 + a), ALU.mult).then_inc(g["og"], 1)

        def gdn_act(act, s):
            R = slice(RB, P)
            act.wait_ge(col_in, 32)
            done("ea", nc.scalar.activation(ea_col[R], a_col[R], ACT.Exp))
            after(act, "z")
            done("e", nc.scalar.activation(e_buf[R], z_buf[R], ACT.Exp))
            after(act, "e")
            done("l", nc.scalar.activation(l_buf[R], e_buf[R], ACT.Ln, bias=1.0))
            done("sg", nc.scalar.activation(sg[R], ab[R], ACT.Sigmoid))
            for c in range(2 * HA):
                if c >= 2:
                    act.wait_ge(g["summed"], c - 1)
                nc.scalar.activation(sqk[:, c % 2], qkv[:, c], ACT.Square).then_inc(g["square"], 1)
            act.wait_ge(g["summed"], 2 * HA)
            done("std16", nc.scalar.activation(halves(std16[0:2 * HA]), TILE[0][0:2 * HA], ACT.Sqrt, bias=eps[0:2 * HA]))
            after(act, "cst0", "cst1", "kdx0", "kdx1")
            done("ex0", nc.scalar.activation(est[:, 0:C_S], cst[:, 0:C_S], ACT.Exp))
            done("ex1", nc.scalar.activation(est[0:TS, C_S:], cst[0:TS, C_S:], ACT.Exp))
            done("exk0", nc.scalar.activation(kdc[:, 0:C_E], kdc[:, 0:C_E], ACT.Exp))
            done("exk1", nc.scalar.activation(kdc[0:TS, C_E:], kdc[0:TS, C_E:], ACT.Exp))
            with act.Fori(0, HA // 2) as hp:
                for a in range(2):
                    L = lane[a]
                    act.wait_ge(g["bc"], hp * 8 + (4 * a + 3))
                    nc.scalar.activation(L["eb"][:], bank(4 * a + 2), ACT.Exp).then_inc(g["eb"], 1)
                    nc.scalar.activation(L["vc"][:], dyn(qkv, hp * 2 + (2 * HA + a))[:, 0:TP], ACT.Copy).then_inc(g["vcopy"], 1)
                for a in range(2):
                    L = lane[a]
                    act.wait_ge(g["dsub"], hp * 2 + (a + 1))
                    nc.scalar.activation(L["dx"][:], L["dx"][:], ACT.Exp).then_inc(g["dexp"], 1)
                for a in range(2):
                    act.wait_ge(g["xtr"], hp * 2 + (a + 1))
                    act.wait_ge(g["vt"], hp * 2 + (a + 1))
                    nc.scalar.activation(lane[a]["x"][:], bank(4 * a + 3), ACT.Copy).then_inc(g["xc"], 1)
                for level in range(1, LEVELS):
                    for a in range(2):
                        act.wait_ge(g["am"], cnt(hp, a, LEVELS - 1, level - 1))
                        nc.scalar.activation(lane[a]["A"][:], bank(4 * a), ACT.Copy).then_inc(g["acp"], 1)
                for a in range(2):
                    act.wait_ge(g["wm"], hp * 2 + (a + 1))
                    nc.scalar.activation(lane[a]["wn"][:], bank(4 * a + 3), ACT.Copy, scale=-1.0).then_inc(g["wn"], 1)
                for i in range(PT):
                    for a in range(2):
                        act.wait_ge(g["vm"], cnt(hp, a, PT, i))
                        nc.scalar.activation(lane[a]["vn"][:], ps[:, 4 * a, 0:P], ACT.Copy).then_inc(g["vcp"], 1)
                    for a in range(2):
                        act.wait_ge(g["om"], cnt(hp, a, PT, i))
                        nc.scalar.activation(dyn(qkv, hp * 2 + a)[:, i * P:(i + 1) * P], ps[:, 4 * a + 1, 0:P], ACT.Copy
                                             ).then_inc(g["ocp"], 1)
            after(act, "bc_s")
            done("eb_s", nc.scalar.activation(eb_s[:], by_head(bank(2)), ACT.Exp))
            after(act, "dneg_s")
            done("dexp_s", nc.scalar.activation(dx_s[0:TS], dx_s[0:TS], ACT.Exp))
            after(act, "xtr_s")
            done("xc_s", nc.scalar.activation(x_s[0:TS], by_head(bank(2)[0:TS]), ACT.Copy))
            for level in range(1, S_LEVELS):
                after(act, f"am{level}_s")
                done(f"acp{level}_s", nc.scalar.activation(A_s[0:TS], by_head(bank(3)[0:TS]), ACT.Copy))
            after(act, "wm_s")
            done("wn_s", nc.scalar.activation(wq_s[:, :, 0:TD], bank(2).rearrange("p (x t) -> p x t", t=TD), ACT.Copy, scale=-1.0))
            after(act, "ut_s")
            done("utc_s", nc.scalar.activation(vnT_s[:], by_head(bank(3)), ACT.Copy))
            after(act, "osum_s", f"su{HA - 1}_s")
            for h in range(HA):
                if h >= 2:
                    act.wait_ge(g["osum"], h - 1)
                nc.scalar.activation(osq[:, h % 2], qkv[:, h], ACT.Square).then_inc(g["osq"], 1)
            act.wait_ge(g["osum"], HA)
            done("ostd", nc.scalar.activation(halves(ostd[0:HA]), TILE[0][0:HA], ACT.Sqrt, bias=eps[0:HA], scale=1.0 / DH))
            after(act, "orec", f"upd{HA - 1}_s")
            with act.Fori(0, HA // 2) as hp:
                for a in range(2):
                    act.wait_ge(g["bco"], hp * 2)
                    nc.scalar.activation(omask[0:HA, a], rows[0:HA], ACT.Copy, scale=e32[0:HA, ds(hp * 2 + a, 1)]
                                         ).then_inc(g["mask"], 1)
                for a in range(2):
                    act.wait_ge(g["og"], hp * 2 + (a + 1))
                    nc.scalar.activation(hid_hi[:, ds(hp * 2 + a, 1)], og[:, a:a + 1], ACT.Copy).then_inc(hid_hi_done, 1)

        def gdn_dve(dve, s):
            R = slice(RB, P)
            tt, stt = nc.vector.tensor_tensor, nc.vector.scalar_tensor_tensor
            for par in range(2):
                dve.wait_ge(tok_ev[par], (s.n["tok"] + 1 - par) // 2)
            dve.wait_ge(stored, 32)
            dve.wait_ge(evac[0], s.n["unit"])
            dve.wait_ge(col_in, 32)
            done("z", nc.vector.tensor_scalar(z_buf[R], ab[R], dt_col[R], SOFTPLUS_CAP, ALU.add, ALU.min))
            after(dve, "l")
            done("sp", stt(z_buf[R], ab[R], dt_col[R], l_buf[R], ALU.add, ALU.max))
            after(dve, "sp", "sg")
            done("g", nc.vector.tensor_scalar(ab[R], z_buf[R], ea_col[R], -1.0, ALU.mult, ALU.mult))
            after(dve, "tok_ab")
            done("tokc0", nc.vector.tensor_copy(tokc[:, 0:PT], bank(4)[:, 0:PT * 2 * NR].rearrange("p (i c) -> p i c", i=PT)))
            done("tokc1", nc.vector.tensor_copy(tokc[0:TS, PT], bank(4)[0:TS, PT * 2 * NR:NT * 2 * NR]))
            after(dve, "std16")
            done("rec", nc.vector.reciprocal(rows[0:2 * HA], std16[0:2 * HA]))
            after(dve, "gc_all")
            for name, p0 in (("gc", 32), ("be", 64)):
                done("rows_" + name, nc.vector.tensor_copy(rows[p0:p0 + HA, 0:TP], bank(6)[p0:p0 + HA]))
                done(f"rows_{name}s", nc.vector.tensor_copy(rows[p0:p0 + HA, TP:T], bank(7)[p0:p0 + HA, 0:TS]))
            done("cst0", nc.vector.tensor_copy(cst[:, 0:C_S], bank(5)[:, 0:C_S]))
            done("cst1", nc.vector.tensor_copy(cst[0:TS, C_S:], bank(5)[0:TS, C_S:C_S + 2 * HA]))
            after(dve, "cst0", "cst1")
            done("kdx0", tt(kdc[:, 0:C_E], cst[:, C_E:C_S], cst[:, 0:C_E], ALU.subtract))
            done("kdx1", tt(kdc[0:TS, C_E:], cst[0:TS, C_S + HA:], cst[0:TS, C_S:C_S + HA], ALU.subtract))
            after(dve, "ex0", "ex1")
            done("be0", tt(bec[:, 0:C_E].rearrange("p (i h) -> p i h", h=HA), tokc[:, 0:PT, C_B:C_B + HA],
                           est[:, 0:C_E].rearrange("p (i h) -> p i h", h=HA), ALU.mult))
            done("be1", tt(bec[0:TS, C_E:], tokc[0:TS, PT, C_B:C_B + HA], est[0:TS, C_S:C_S + HA], ALU.mult))
            after(dve, "be0", "be1", "exk0", "exk1")

            def col(c, at):
                return c.rearrange("p (i h) -> p i h", h=HA)[:, :, ds(at, 1)].to_broadcast((P, PT, P))

            with dve.Fori(0, HA // 2) as hp:
                for a in range(2):
                    L, h, n = lane[a], hp * 2 + a, hp * 2 + (a + 1)
                    cols = lambda t: t.rearrange("p i n -> p (i n)")
                    dve.wait_ge(g["bc"], hp * 8 + (4 * a + 1))
                    stt(cols(L["qnT"][:]), dyn(qkv, h)[:, 0:TP], DH ** -0.5, bank(4 * a), ALU.mult, ALU.mult).then_inc(g["qn"], 1)
                    dve.wait_ge(g["bc"], hp * 8 + (4 * a + 2))
                    tt(cols(L["knT"][:]), dyn(qkv, h + HA)[:, 0:TP], bank(4 * a + 1), ALU.mult).then_inc(g["kn"], 1)
                    dve.wait_ge(g["bc"], hp * 8 + (4 * a + 4))
                    dve.wait_ge(g["eb"], n)
                    for i in range(PT):
                        last = stt(L["dx"][:, i], bank(4 * a + 2)[:, i * P:(i + 1) * P], cst[:, ds(hp * 2 + (i * HA + a), 1)],
                                   neg_le[:], ALU.subtract, ALU.add)
                    last.then_inc(g["dsub"], 1)
                    dve.wait_ge(g["kn"], n)
                    tt(cols(L["kbT"][:]), cols(L["knT"][:]), bank(4 * a + 3), ALU.mult).then_inc(g["kb"], 1)
                    dve.wait_ge(g["qn"], n)
                    tt(L["qdT"][:], L["qnT"][:], L["eb"][:], ALU.mult).then_inc(g["qd"], 1)
                for a in range(2):
                    L, h, n = lane[a], hp * 2 + a, hp * 2 + (a + 1)
                    t4 = lambda b: b.rearrange("p (i n) -> p i n", i=PT)
                    dve.wait_ge(g["kk"], n)
                    dve.wait_ge(g["dexp"], n)
                    dve.wait_ge(g["qd"], n)
                    tt(L["mt"][:], t4(bank(4 * a)), L["dx"][:], ALU.mult).then_inc(g["mt"], 1)
                    dve.wait_ge(g["qk"], n)
                    tt(L["qkm"][:], t4(bank(4 * a + 1)), L["dx"][:], ALU.mult).then_inc(g["qkm"], 1)
                    dve.wait_ge(g["kt"], n)
                    tt(L["kbg"][:], t4(bank(4 * a + 3)), col(bec[:, 0:C_E], h), ALU.mult).then_inc(g["kbg"], 1)
                    tt(L["kd"][:], t4(bank(4 * a + 3)), col(kdc[:, 0:C_E], h), ALU.mult).then_inc(g["kd"], 1)
                    dve.wait_ge(g["vt"], n)
                    tt(L["vb"][:], t4(bank(4 * a + 2)), tokc[:, 0:PT, ds(hp * 2 + (C_B + a), 1)].to_broadcast((P, PT, P)),
                       ALU.mult).then_inc(g["vb"], 1)
                for level in range(LEVELS):
                    for a in range(2):
                        L = lane[a]
                        if level == 0:
                            dve.wait_ge(g["mo"], cnt(hp, a, LEVELS, 0))
                            tt(L["xt"][:], ident[:].unsqueeze(1).to_broadcast((P, PT, P)), L["mo"][:], ALU.subtract
                               ).then_inc(g["xtu"], 1)
                            continue
                        if level < LEVELS - 1:
                            dve.wait_ge(g["dm"], cnt(hp, a, LEVELS - 2, level - 1))
                            tt(L["x"][:], L["x"][:], t4(bank(4 * a + 1)), ALU.subtract).then_inc(g["xu"], 1)
                        dve.wait_ge(g["dtm"], cnt(hp, a, LEVELS - 1, level - 1))
                        tt(L["xt"][:], L["xt"][:], t4(bank(4 * a + 2)), ALU.subtract).then_inc(g["xtu"], 1)
                for i in range(PT):
                    for a in range(2):
                        if i == 0:
                            dve.wait_ge(s_out, hp * 32)
                        dve.wait_ge(g["sm"], cnt(hp, a, PT, i))
                        if i == 0:
                            nc.vector.tensor_copy(state[:, a], ps[:, 4 * a + 2, 0:P]).then_inc(g["su"], 1)
                        else:
                            stt(state[:, a], state[:, a], est[:, ds(hp * 2 + (C_E + i * HA + a), 1)], ps[:, 4 * a + 2, 0:P],
                                ALU.mult, ALU.add).then_inc(g["su"], 1)
            S = slice(0, TS)

            def spread(name, dst, p0, n, e0):
                done(name, tt(dst[p0:p0 + n], rows[p0:p0 + n, TP:T].unsqueeze(1).to_broadcast((n, HA, TS)),
                              e32[p0:p0 + n, e0:e0 + HA].unsqueeze(2).to_broadcast((n, HA, TS)), ALU.mult))

            def wide(cols):
                return cols.unsqueeze(2).to_broadcast((TS, HA, DH))

            dve.wait_ge(g["ocp"], HA * PT)
            spread("mq_s", dx_s, 0, 2 * HA, 0)
            spread("mk_s", mt_s, 0, 2 * HA, HA)
            spread("mg_s", dx_s, 32, HA, 0)
            spread("mb_s", dx_s, 64, HA, 0)
            after(dve, "bc_s")
            done("qn_s", stt(qn_s[:], qkv[:, 0:HA, TP:T], DH ** -0.5, by_head(bank(0)), ALU.mult, ALU.mult))
            done("kn_s", tt(kn_s[:], qkv[:, HA:2 * HA, TP:T], by_head(bank(1)), ALU.mult))
            after(dve, "kn_s")
            done("kb_s", tt(kb_s[:], kn_s[:], by_head(bank(3)), ALU.mult))
            after(dve, "eb_s", "qn_s")
            x3 = lambda t: t.rearrange("p h (b t) -> p (h b) t", t=TD)
            done("qd_s", tt(wq_s[:, :, TD:], x3(qn_s[:]), x3(eb_s[:]), ALU.mult))
            done("dsub_s", tt(dx_s[S], by_head(bank(2)[S]), cst[S, C_S:C_S + HA].unsqueeze(2).to_broadcast((TS, HA, TS)), ALU.subtract))
            after(dve, "dsub_s")
            done("dneg_s", tt(dx_s[S], dx_s[S], neg_le_s[:].unsqueeze(1).to_broadcast((TS, HA, TS)), ALU.add))
            after(dve, "dexp_s", "kk_s")
            done("mt_s", tt(mt_s[S], by_head(bank(4)[S]), dx_s[S], ALU.mult))
            after(dve, "qk_s")
            done("qkm_s", tt(qkm_s[S], by_head(bank(5)[S]), dx_s[S], ALU.mult))
            after(dve, "vt_s")
            done("vb_s", tt(vb_s[:], bank(6, 2)[S].rearrange("p (h d) -> p h d", d=DH), wide(tokc[S, PT, C_B:C_B + HA]), ALU.mult))
            after(dve, "kt_s")
            done("kbg_s", tt(kbg_s[:], bank(0, 2)[S].rearrange("p (h d) -> p h d", d=DH), wide(bec[S, C_E:]), ALU.mult))
            done("kd_s", tt(kd_s[:], bank(0, 2)[S].rearrange("p (h d) -> p h d", d=DH), wide(kdc[S, C_E:]), ALU.mult))
            done("gts_s", nc.vector.tensor_copy(gts[:].unsqueeze(2), x3(eb_s[:])[:, :, TD - 1:TD]))
            after(dve, "mt_s", "qkm_s")
            for level in range(S_LEVELS):
                if level:
                    after(dve, "xt0_s" if level == 1 else f"am{level - 1}_s")
                done(f"mo{level}_s", tt(mo_s[S], mt_s[S], lm[S, level, 0:TS].unsqueeze(1).to_broadcast((TS, HA, TS)), ALU.mult))
                if level == 0:
                    after(dve, "mo0_s")
                    done("xt0_s", tt(xt_s[S], ident[S, 0:TS].unsqueeze(1).to_broadcast((TS, HA, TS)), mo_s[S], ALU.subtract))
                    continue
                if level < S_LEVELS - 1:
                    after(dve, f"dm{level}_s")
                    done(f"xu{level}_s", tt(x_s[S], x_s[S], by_head(bank(4)[S]), ALU.subtract))
                after(dve, f"dtm{level}_s")
                done(f"xtu{level}_s", tt(xt_s[S], xt_s[S], by_head(bank(5)[S]), ALU.subtract))
            after(dve, "sw_s", "utc_s")
            sw = bank(6, 2).rearrange("p (x t) -> p x t", t=2 * TD)
            done("vnt_s", tt(x3(vnT_s[:]), sw[:, :, 0:TD], x3(vnT_s[:]), ALU.add))
            done("os_s", nc.vector.tensor_copy(x3(oT_s[:]), sw[:, :, TD:]))
            after(dve, "vtr_s")
            done("vnc_s", nc.vector.tensor_copy(vn_s[:], bank(0, 2)[S].rearrange("p (h d) -> p h d", d=DH)))
            after(dve, "om_s", "os_s")
            done("osum_s", tt(qkv[:, 0:HA, TP:T], by_head(bank(2)), oT_s[:], ALU.add))
            for h in range(HA):
                after(dve, "vnc_s", "ut_s")
                if h >= 2:
                    after(dve, f"su{h - 2}_s")
                mine = same[:].rearrange("p (b t) -> p b t", t=TD)[:, :, 0:1].to_broadcast((TS, NB, DH))
                done(f"vnm{h}_s", tt(vnm[h % 2][:], vn_s[:, h:h + 1].to_broadcast((TS, NB, DH)), mine, ALU.mult))
                if h:
                    update(dve, h - 1)
            update(dve, HA - 1)
            after(dve, "ostd")
            done("orec", nc.vector.reciprocal(rows[0:HA], ostd[0:HA]))
            dve.wait_ge(qs_out, 32 * HA)
            with dve.Fori(0, HA // 2) as hp:
                for a in range(2):
                    dve.wait_ge(g["bco"], hp * 2 + (a + 1))
                    dve.wait_ge(g["og"], hp * 2)
                    stt(halves(of[:, a]), halves(dyn(qkv, hp * 2 + a)), gain[:, ON:ON + 1], TILE[a], ALU.mult, ALU.mult
                        ).then_inc(g["of"], 1)
                for a in range(2):
                    dve.wait_ge(hid_hi_done, hp * 2 + (s.n["hid"] + a + 1))
                    tt(hid_lo[:, ds(hp * 2 + a, 1)], og[:, a:a + 1], hid_hi[:, ds(hp * 2 + a, 1)].bitcast(F32), ALU.subtract
                       ).then_inc(hid_done, 1)

        def update(dve, h):
            after(dve, f"su{h}_s", f"stg{h}_s")
            new = bank(4 + 2 * (h % 2), 2).rearrange("p (c b d) -> p c b d", c=2, d=DH)
            done(f"upd{h}_s", nc.vector.tensor_tensor(st(h), new, st(h), ALU.add))

        def gdn_pe(pe, s):
            mm, tr = nc.tensor.matmul, nc.tensor.transpose

            def col(n, i):
                return ps[:, n, i * P:(i + 1) * P]

            pe.wait_ge(evac[0], s.n["unit"])
            pe.wait_ge(evac[1], s.n["eb"])
            for c in range(2 * HA):
                pe.wait_ge(g["square"], c + 1)
                for half in range(2):
                    last = mm(TILE[0][0:2 * HA, half], hot[:, 15 - c:15 - c + 2 * HA], sqk[:, c % 2, half * HC:(half + 1) * HC],
                              start=c == 0, stop=c == 2 * HA - 1)
                last.then_inc(g["summed"], 1)
            after(pe, "g", "sg")
            for i in range(NT):
                n = P if i < PT else TS
                for half, src in enumerate((ab, sg)):
                    last = tr(ps[0:n, 4, (2 * i + half) * NR:(2 * i + half + 1) * NR], src[RB:P, i * P:i * P + n], ident[RB:P, RB:P])
            done("tok_ab", last)
            after(pe, "tokc0", "tokc1")
            gp = tokc[:, 0:PT, C_G:C_G + HA]
            gs_ = tokc[0:TS, PT, C_G:C_G + HA]
            mm(ps[:, 5, 0:C_E], triu[:], gp, start=True, stop=True)
            mm(ps[:, 5, C_E:C_S], ones[:], gp, start=True, stop=True)
            mm(ps[0:TS, 5, C_S:C_S + HA], triu_s[:], gs_, start=True, stop=True)
            mm(ps[0:TS, 5, C_S + HA:C_S + 2 * HA], same[:], gs_, start=True, stop=True)
            for p0, c0, tri, tri_s in ((32, C_G, triu, triu_s), (64, C_B, ident, ident[0:TS, 0:TS])):
                for i in range(PT):
                    mm(ps[p0:p0 + HA, 6, i * P:(i + 1) * P], tokc[:, i, c0:c0 + HA], tri[:], start=True, stop=True)
                last = mm(ps[p0:p0 + HA, 7, 0:TS], tokc[0:TS, PT, c0:c0 + HA], tri_s[:] if tri_s is triu_s else tri_s,
                          start=True, stop=True)
            done("gc_all", last)
            after(pe, "rec", "rows_bes", "cst1")
            with pe.Fori(0, HA // 2) as hp:
                for a in range(2):
                    pe.wait_ge(g["sel"], hp * 4 + (2 * a + 2))
                    if a == 0:
                        pe.wait_ge(g["vcp"], hp * 8)
                        pe.wait_ge(g["ocp"], hp * 8)
                        pe.wait_ge(g["su"], hp * 8)
                    for b, (p0, n, q) in enumerate(((0, 2 * HA, 0), (0, 2 * HA, 1), (32, HA, 0), (64, HA, 0))):
                        mm(bank(4 * a + b), sel[p0:p0 + n, a, q], rows[p0:p0 + n, 0:TP], start=True, stop=True).then_inc(g["bc"], 1)
                for a in range(2):
                    L, n = lane[a], hp * 2 + (a + 1)
                    pe.wait_ge(g["kb"], n)
                    for i in range(PT):
                        last = mm(col(4 * a, i), L["knT"][:, i], L["kbT"][:, i], start=True, stop=True)
                    last.then_inc(g["kk"], 1)
                    for i in range(PT):
                        last = mm(col(4 * a + 1, i), L["knT"][:, i], L["qnT"][:, i], start=True, stop=True)
                    last.then_inc(g["qk"], 1)
                    for i in range(PT):
                        last = tr(col(4 * a + 3, i), L["knT"][:, i], ident[:])
                    last.then_inc(g["kt"], 1)
                    pe.wait_ge(g["vcopy"], n)
                    pe.wait_ge(g["eb"], n)
                    pe.wait_ge(g["dsub"], n)
                    for i in range(PT):
                        last = tr(col(4 * a + 2, i), L["vc"][:, i], ident[:])
                    last.then_inc(g["vt"], 1)
                for a in range(2):
                    pe.wait_ge(g["xtu"], cnt(hp, a, LEVELS, 0))
                    pe.wait_ge(g["kd"], hp * 2 + (a + 1))
                    for i in range(PT):
                        last = tr(col(4 * a + 3, i), lane[a]["xt"][:, i], ident[:])
                    last.then_inc(g["xtr"], 1)
                for level in range(1, LEVELS):
                    for a in range(2):
                        L = lane[a]
                        pe.wait_ge(g["mo"], cnt(hp, a, LEVELS, level))
                        if level == 1:
                            pe.wait_ge(g["xc"], hp * 2 + (a + 1))
                            pe.wait_ge(g["mt"], hp * 2 + (a + 1))
                        else:
                            pe.wait_ge(g["xu"], cnt(hp, a, LEVELS - 2, level - 2))
                        for i in range(PT):
                            last = mm(col(4 * a, i), L["mo"][:, i], L["x"][:, i], start=True, stop=True)
                        last.then_inc(g["am"], 1)
                    for a in range(2):
                        L = lane[a]
                        pe.wait_ge(g["acp"], cnt(hp, a, LEVELS - 1, level - 1))
                        if level == 1:
                            pe.wait_ge(g["vb"], hp * 2 + (a + 1))
                        pe.wait_ge(g["xtu"], cnt(hp, a, LEVELS, level - 1))
                        if level < LEVELS - 1:
                            for i in range(PT):
                                last = mm(col(4 * a + 1, i), L["xt"][:, i], L["A"][:, i], start=True, stop=True)
                            last.then_inc(g["dm"], 1)
                        for i in range(PT):
                            last = mm(col(4 * a + 2, i), L["A"][:, i], L["xt"][:, i], start=True, stop=True)
                        last.then_inc(g["dtm"], 1)
                for a in range(2):
                    L = lane[a]
                    pe.wait_ge(g["xtu"], cnt(hp, a, LEVELS, LEVELS - 1))
                    for i in range(PT):
                        last = mm(col(4 * a + 3, i), L["kbg"][:, i], L["xt"][:, i], start=True, stop=True)
                    last.then_inc(g["wm"], 1)
                for i in range(PT):
                    for a in range(2):
                        L = lane[a]
                        if i:
                            pe.wait_ge(g["vcp"], cnt(hp, a, PT, i - 1))
                            pe.wait_ge(g["su"], cnt(hp, a, PT, i - 1))
                        mm_last = mm(ps[:, 4 * a, 0:P], L["xt"][:, i], L["vb"][:, i], start=True, stop=i == 0)
                        if i:
                            if i == 1:
                                pe.wait_ge(g["wn"], hp * 2 + (a + 1))
                            mm_last = mm(ps[:, 4 * a, 0:P], L["wn"][:, i], state[:, a], start=False, stop=True)
                        mm_last.then_inc(g["vm"], 1)
                    for a in range(2):
                        L = lane[a]
                        if i:
                            pe.wait_ge(g["ocp"], cnt(hp, a, PT, i - 1))
                            mm(ps[:, 4 * a + 1, 0:P], state[:, a], L["qdT"][:, i], start=True, stop=False)
                        pe.wait_ge(g["vcp"], cnt(hp, a, PT, i))
                        mm(ps[:, 4 * a + 1, 0:P], L["vn"][:], L["qkm"][:, i], start=i == 0, stop=True).then_inc(g["om"], 1)
                        mm(ps[:, 4 * a + 2, 0:P], L["kd"][:, i], L["vn"][:], start=True, stop=True).then_inc(g["sm"], 1)
            after(pe, "mq_s", "mk_s", "mg_s", "mb_s")
            for b, (src, p0, n) in enumerate(((dx_s, 0, 2 * HA), (mt_s, 0, 2 * HA), (dx_s, 32, HA), (dx_s, 64, HA))):
                last = mm(bank(b), ones[p0:p0 + n], src[p0:p0 + n].rearrange("p h t -> p (h t)"), start=True, stop=True)
            done("bc_s", last)

            def heads(name, n, lhs, rhs, w=TS, rows_=TS, transposed=False):
                for h in range(HA):
                    out = bank(n, 2 if w == DH else 1)[0:rows_, h * w:(h + 1) * w]
                    if transposed:
                        last = tr(out, lhs(h), ident[0:lhs(h).shape[0], 0:lhs(h).shape[0]])
                    else:
                        last = mm(out, lhs(h), rhs(h), start=True, stop=True)
                done(name, last)

            after(pe, "kb_s", "qn_s")
            heads("kk_s", 4, lambda h: kn_s[:, h], lambda h: kb_s[:, h])
            heads("qk_s", 5, lambda h: kn_s[:, h], lambda h: qn_s[:, h])
            heads("vt_s", 6, lambda h: qkv[:, 2 * HA + h, TP:T], None, w=DH, transposed=True)
            heads("kt_s", 0, lambda h: kn_s[:, h], None, w=DH, transposed=True)
            after(pe, "xt0_s", "eb_s", "dsub_s")
            heads("xtr_s", 2, lambda h: xt_s[0:TS, h], None, transposed=True)
            for level in range(1, S_LEVELS):
                after(pe, f"mo{level}_s", "xc_s" if level == 1 else f"xu{level - 1}_s")
                heads(f"am{level}_s", 3, lambda h: mo_s[0:TS, h], lambda h: x_s[0:TS, h])
                after(pe, f"acp{level}_s", f"xtu{level - 1}_s" if level > 1 else "xt0_s", "mt_s", "qkm_s")
                if level < S_LEVELS - 1:
                    heads(f"dm{level}_s", 4, lambda h: xt_s[0:TS, h], lambda h: A_s[0:TS, h])
                heads(f"dtm{level}_s", 5, lambda h: A_s[0:TS, h], lambda h: xt_s[0:TS, h])
            after(pe, f"xtu{S_LEVELS - 1}_s", "kbg_s", "vb_s", "kd_s")
            heads("wm_s", 2, lambda h: kbg_s[:, h], lambda h: xt_s[0:TS, h], rows_=P)
            heads("ut_s", 3, lambda h: vb_s[:, h], lambda h: xt_s[0:TS, h], rows_=P)
            after(pe, "wn_s", "qd_s")
            pe.wait_ge(st_in, 32 * HA)
            sw = bank(6, 2).rearrange("p (x t) -> p x t", t=2 * TD)
            for h in range(HA):
                for b in range(NB):
                    last = mm(sw[:, h * NB + b], st1(h, b), wq_s[:, h * NB + b], start=True, stop=True)
            done("sw_s", last)
            after(pe, "vnt_s")
            heads("vtr_s", 0, lambda h: vnT_s[:, h], None, w=DH, transposed=True)
            after(pe, "vnc_s")
            heads("om_s", 2, lambda h: vn_s[:, h], lambda h: qkm_s[0:TS, h], rows_=P)
            after(pe, "os_s", f"xtu{S_LEVELS - 1}_s")
            for h in range(HA):
                after(pe, f"vnm{h}_s")
                if h >= 2:
                    after(pe, f"upd{h - 2}_s")
                for half in range(2):
                    last = mm(bank(4 + 2 * (h % 2) + half), kd_s[:, h], vnm[h % 2][:, half * PT:(half + 1) * PT].rearrange("p b d -> p (b d)"),
                              start=True, stop=True)
                done(f"su{h}_s", last)
            after(pe, "vnc_s")
            for h in range(HA):
                pe.wait_ge(g["osq"], h + 1)
                for half in range(2):
                    last = mm(TILE[0][0:HA, half], hot[:, 15 - h:15 - h + HA], osq[:, h % 2, half * HC:(half + 1) * HC],
                              start=h == 0, stop=h == HA - 1)
                last.then_inc(g["osum"], 1)
            after(pe, "ostd", "osum_s")
            with pe.Fori(0, HA // 2) as hp:
                for a in range(2):
                    pe.wait_ge(g["mask"], hp * 2 + (a + 1))
                    pe.wait_ge(g["of"], hp * 2)
                    for half in range(2):
                        last = mm(TILE[a][:, half], ones[0:HA], omask[0:HA, a, half * HC:(half + 1) * HC], start=True, stop=True)
                    last.then_inc(g["bco"], 1)
            pe.wait_ge(g["of"], HA)

        NP = HB // 2
        NU = 4 * PT
        W = [TP - P * (PT - 1 - j) for j in range(PT)]
        AT = [sum(W[:j]) for j in range(PT)]
        WALL = sum(W)
        HS = 2 * TS
        PGC = HB * TD
        at = {n: sem("at_" + n) for n in (
            "zero", "q_sample", "new_out", "k_tr", "z_page", "zb_page", "zc_page", "e_page", "l_page", "max_page", "r_page",
            "sub_page", "att_page", "o_page", "o_sum", "o_hi_page", "o_lo_page",
            "copied", "z", "zb", "zc", "e", "l", "max", "keep", "mask", "r", "sub", "att", "o_head", "o_hi0", "o_lo0")}
        k_page_in = sem("k_page_in")
        v_page_in = sem("v_page_in")
        k_ev = [sem("k_ev_scalar"), sem("k_ev_vector")]

        r = Region(hx0, hx1)
        q_blocks = r.take("q_blocks", [P, NP, 2, NB, TD])
        k_heads = r.take("k_heads", [P, 2, TP])
        q_heads = r.take("q_heads", [P, 2, TP])
        v_heads = r.take("v_heads", [P, 2, PT, P])
        zb = r.take("zb", [P, 2, WALL])
        ls = r.take("ls", [P, 2, WALL])
        r = Region(scratch0, hx0)
        k_page = [r.take(f"k_page{n}", [P, D]) for n in range(NPG)]
        v_page = [r.take("v_page0", [P, D])]
        o_sum = r.take("o_sum", [P, NP, TD])
        r = Region(tail1, room)
        v_page.append(r.take("v_page1", [P, D]))
        zb_page = r.take("zb_page", [P, NPG, PGC])
        ls_page = r.take("ls_page", [P, NPG, PGC])
        zb_new = Region(r.at, room).take("zb_new", [TS, HB, TS])
        kT_page = r.take("kT_page", [P, NPG, NP, P])
        r = Region(norm0, norm1)
        ls_new = r.take("ls_new", [TS, HB, TS])
        o_new = r.take("o_new", [P, NP, NB, TD])

        def unit_of(turn, n, last):
            if n < NU:
                return turn * NU + n, n // PT, n % PT
            return None if last else (turn * NU + n, n // PT - PT, n % PT)

        def turns(eng, body):
            with eng.Fori(0, NP // 2 - 1) as turn:
                body(turn, False)
            body(NP // 2 - 1, True)

        def attend_sp(sp, s):
            sp.wait_ge(small_in, 32)
            sp.wait_ge(ssum_done, KD * s.n["sum"])
            sp.wait_ge(hid_done, s.n["hid"])
            sp.wait_ge(p_done, 2 * PK)
            for b in range(NB):
                number = [sp.value_load(pages[0:1, n:n + 1], min_val=0, max_val=NPHYS - 1) for n in range(b * NPG, (b + 1) * NPG)]
                if b:
                    sp.wait_ge(at["k_tr"], 4 * b)
                for n in range(NPG):
                    sp.dma_start(k_page[n][:], A["cache_k"][ds(number[n], 1)].squeeze(0).rearrange("s h d -> s (h d)")
                                 ).then_inc(k_page_in, 16)
                if b:
                    sp.wait_ge(at["o_page"], b)
                for n in range(NPG):
                    sp.dma_start(v_page[n][:], A["cache_v"][ds(number[n], 1)].squeeze(0).rearrange("s h d -> s (h d)")
                                 ).then_inc(v_page_in, 16)

        def attend_pool(pool, s):
            pool.wait_ge(small_in, 32)
            pool.wait_ge(tile_done, 2 * s.n["unit"])
            nc.gpsimd.memset(q_blocks[:], 0.0).then_inc(at["zero"], 1)
            pool.wait_ge(at["zero"], 1)
            for m in range(2):
                pool.wait_ge(evac[m], s.n["unit"] if m == 0 else s.n["eb"])
            for a in range(2):
                rows_ = slice(a * HD, (a + 1) * HD)
                nc.gpsimd.tensor_copy(q_blocks[rows_, :, a].rearrange("p f b t -> p f (b t)"), qT[rows_, :, TP:T]
                                      ).then_inc(at["q_sample"], 1)

            def copies(pair, par):
                nc.gpsimd.tensor_copy(k_heads[:, par:par + 1], kT[:, ds(pair, 1), 0:TP]).then_inc(at["copied"], 1)
                nc.gpsimd.tensor_copy(q_heads[:, par:par + 1], qT[:, ds(pair, 1), 0:TP]).then_inc(at["copied"], 1)
                nc.gpsimd.tensor_copy(v_heads[:, par], v_tok[:, 0:PT, ds(pair * P, P)]).then_inc(at["copied"], 1)
                nc.gpsimd.tensor_copy(bias_c[:, par], bias_b[:, ds(pair * 2, 2)]).then_inc(at["copied"], 1)

            def masks(u, c, j):
                a = c % 2
                d = slice(AT[j], AT[j] + P)
                pool.wait_ge(at["max"], u + 1)
                nc.gpsimd.tensor_tensor(ls[:, a, d], ls[:, a, d], lt[:], ALU.mult).then_inc(at["keep"], 1)
                nc.gpsimd.tensor_tensor(zb[:, a, d], zb[:, a, d], neg_lt[:], ALU.add).then_inc(at["mask"], 1)

            pool.wait_ge(at["q_sample"], 2)
            copies(0, 0)
            for n in range(2):
                masks(n, 0, n)

            def turn_(turn, last):
                pool.wait_ge(at["o_head"], turn * PT)
                copies(turn * 2 + 1, 1)
                for n in range(NU):
                    if n == 8 and not last:
                        pool.wait_ge(at["o_head"], turn * PT + 2)
                        copies(turn * 2 + 2, 0)
                    if unit := unit_of(turn, n + 2, last):
                        masks(*unit)
            turns(pool, turn_)
            pool.wait_ge(at["o_lo_page"], 2 * NB)

        def attend_act(act, s):
            nc.scalar.preload_act_table_set("natural_log_exp_and_others")
            after(act, "zcn")
            done("en", nc.scalar.activation(ls_new[:], ls_new[:], ACT.Exp))
            after(act, "en")
            done("ln", nc.scalar.activation(ls_new[:], ls_new[:], ACT.Ln, bias=1.0))
            def scores(unit):
                if unit:
                    u, c, j = unit
                    act.wait_ge(at["z"], u + 1)
                    nc.scalar.activation(zb[:, c % 2, AT[j]:AT[j] + W[j]], ps[:, 4 + j % 2, 0:W[j]], ACT.Identity,
                                         bias=bias_c[:, c // 2, c % 2:c % 2 + 1]).then_inc(at["zb"], 1)

            def logs(unit):
                if unit:
                    u, c, j = unit
                    part = ls[:, c % 2, AT[j]:AT[j] + W[j]]
                    act.wait_ge(at["zc"], u + 1)
                    nc.scalar.activation(part, part, ACT.Exp).then_inc(at["e"], 1)
                    act.wait_ge(at["e"], u + 1)
                    nc.scalar.activation(part, part, ACT.Ln, bias=1.0).then_inc(at["l"], 1)

            def output(turn, c):
                rows_ = slice(c % 2 * HD, (c % 2 + 1) * HD)
                act.wait_ge(at["o_head"], turn * PT + (c + 1))
                nc.scalar.activation(hid_hi[rows_, ds(turn * 2 + c // 2, 1), 0:TP], ps[rows_, c % 2:c % 2 + 1], ACT.Copy
                                     ).then_inc(hid_hi_done if c % 2 else at["o_hi0"], 1)

            def page_step(turn, n):
                r_, n = n // 8, n % 8
                if n in (0, 2):
                    act.wait_ge(at["k_tr"], turn * 8 + (4 * r_ + n + 1))
                    act.wait_ge(at["z_page"], turn * 2 + r_)
                    nc.scalar.activation(kT_page[:, n // 2, 0:NP // 2], ps[:, 6].rearrange("p (k n) -> p k n", n=P), ACT.Copy
                                         ).then_inc(k_ev[0], 1)
                elif n == 5:
                    act.wait_ge(at["zc_page"], turn * 2 + (r_ + 1))
                    nc.scalar.activation(ls_page[:], ls_page[:], ACT.Exp).then_inc(at["e_page"], 1)
                    act.wait_ge(at["e_page"], turn * 2 + (r_ + 1))
                    nc.scalar.activation(ls_page[:], ls_page[:], ACT.Ln, bias=1.0).then_inc(at["l_page"], 1)
                elif n == 6:
                    act.wait_ge(at["sub_page"], turn * 2 + (r_ + 1))
                    nc.scalar.activation(zb_page[:], zb_page[:], ACT.Exp).then_inc(at["att_page"], 1)
                elif n == 7:
                    for a in range(2):
                        rows_ = slice(a * HD, (a + 1) * HD)
                        act.wait_ge(at["o_sum"], turn * 2 + (r_ + 1))
                        nc.scalar.activation(hid_hi[rows_, :, ds(turn * (2 * TD) + (TP + r_ * TD), TD)], o_sum[rows_], ACT.Copy
                                             ).then_inc(at["o_hi_page"], 1)

            def turn_(turn, last):
                for n in range(NU):
                    logs(unit_of(turn, n + 2, last))
                    if n and n % PT == 0:
                        output(turn, n // PT - 1)
                    u, c, j = unit_of(turn, n, last)
                    part = zb[:, c % 2, AT[j]:AT[j] + W[j]]
                    act.wait_ge(at["sub"], u + 1)
                    nc.scalar.activation(part, part, ACT.Exp).then_inc(at["att"], 1)
                    scores(unit_of(turn, n + 3, last))
                    page_step(turn, n)
                output(turn, PT - 1)

            for n in range(2):
                scores((n, 0, n))
            after(act, "subn")
            done("attn", nc.scalar.activation(zb_new[:], zb_new[:], ACT.Exp))
            logs((0, 0, 0))
            scores((2, 0, 2))
            logs((1, 0, 1))
            act.wait_ge(at["q_sample"], 2)
            turns(act, turn_)

        def sample_tiles(a):
            return ps[a * HD:(a + 1) * HD, 0:2].rearrange("p c (f h x) -> p (c f) h x", h=2, x=TS)[:, :, a]

        def attend_dve(dve, s):
            tt = nc.vector.tensor_tensor

            def lowered(bias, n):
                return bias.unsqueeze(2).to_broadcast((bias.shape[0], HB, n))

            dve.wait_ge(small_in, 32)
            after(dve, "zn")
            zn = ps[0:TS, 2:4].rearrange("p c (h x) -> p (c h) x", x=TS)
            done("zbn", tt(zb_new[:], zn, lowered(bias_b[0:TS], TS), ALU.add))
            after(dve, "zbn")
            done("zcn", nc.vector.tensor_scalar(ls_new[:], zb_new[:], SOFTPLUS_CAP, None, ALU.min))
            after(dve, "ln")
            done("maxn", tt(ls_new[:], ls_new[:], zb_new[:], ALU.max))
            after(dve, "maxn")
            done("keepn", tt(ls_new[:], ls_new[:], lt_s[:].unsqueeze(1).to_broadcast((TS, HB, TS)), ALU.mult))
            done("maskn", tt(zb_new[:], zb_new[:], neg_lt_s[:].unsqueeze(1).to_broadcast((TS, HB, TS)), ALU.add))
            def capped(unit):
                if unit:
                    u, c, j = unit
                    at_ = slice(AT[j], AT[j] + W[j])
                    dve.wait_ge(at["zb"], u + 1)
                    nc.vector.tensor_scalar(ls[:, c % 2, at_], zb[:, c % 2, at_], SOFTPLUS_CAP, None, ALU.min).then_inc(at["zc"], 1)

            def softplus(unit):
                if unit:
                    u, c, j = unit
                    at_ = slice(AT[j], AT[j] + W[j])
                    dve.wait_ge(at["l"], u + 1)
                    tt(ls[:, c % 2, at_], ls[:, c % 2, at_], zb[:, c % 2, at_], ALU.max).then_inc(at["max"], 1)

            def output(turn, c):
                rows_ = slice(c % 2 * HD, (c % 2 + 1) * HD)
                tile = ds(turn * 2 + c // 2, 1)
                if c % 2:
                    dve.wait_ge(hid_hi_done, turn * 2 + (s.n["hid"] + c // 2 + 1))
                else:
                    dve.wait_ge(at["o_hi0"], turn * 2 + (c // 2 + 1))
                tt(hid_lo[rows_, tile, 0:TP], ps[rows_, c % 2:c % 2 + 1], hid_hi[rows_, tile, 0:TP].bitcast(F32), ALU.subtract
                   ).then_inc(hid_done if c % 2 else at["o_lo0"], 1)

            def page_step(turn, n):
                r_, n = n // 8, n % 8
                if n in (1, 3):
                    dve.wait_ge(at["k_tr"], turn * 8 + (4 * r_ + n + 1))
                    dve.wait_ge(at["z_page"], turn * 2 + r_)
                    nc.vector.tensor_copy(kT_page[:, n // 2, NP // 2:], ps[:, 6].rearrange("p (k n) -> p k n", n=P)
                                          ).then_inc(k_ev[1], 1)
                elif n == 4:
                    dve.wait_ge(at["z_page"], turn * 2 + (r_ + 1))
                    for pg in range(NPG):
                        last = tt(zb_page[:, pg].rearrange("p (h t) -> p h t", t=TD),
                                  ps[:, 7, pg * PGC:(pg + 1) * PGC].rearrange("p (h t) -> p h t", t=TD), lowered(bias_b[:], TD), ALU.add)
                    last.then_inc(at["zb_page"], 1)
                    dve.wait_ge(at["zb_page"], turn * 2 + (r_ + 1))
                    nc.vector.tensor_scalar(ls_page[:], zb_page[:], SOFTPLUS_CAP, None, ALU.min).then_inc(at["zc_page"], 1)
                elif n == 5:
                    dve.wait_ge(at["l_page"], turn * 2 + (r_ + 1))
                    tt(ls_page[:], ls_page[:], zb_page[:], ALU.max).then_inc(at["max_page"], 1)
                elif n == 6:
                    dve.wait_ge(at["r_page"], turn * 2 + (r_ + 1))
                    tt(zb_page[:], zb_page[:], ps[:, 7, NPG * PGC:].rearrange("p (n x) -> p n x", n=NPG), ALU.subtract
                       ).then_inc(at["sub_page"], 1)
                elif n == 7:
                    dve.wait_ge(at["o_page"], turn * 2 + (r_ + 1))
                    for a in range(2):
                        rows_ = slice(a * HD, (a + 1) * HD)
                        last = tt(o_sum[rows_], ps[rows_, 7, 0:PGC].rearrange("p (f h t) -> p f h t", h=2, t=TD)[:, :, a],
                                  o_new[rows_, :, ds(turn * 2 + r_, 1)].squeeze(2), ALU.add)
                    last.then_inc(at["o_sum"], 1)
                    for a in range(2):
                        rows_ = slice(a * HD, (a + 1) * HD)
                        cols_ = ds(turn * (2 * TD) + (TP + r_ * TD), TD)
                        dve.wait_ge(at["o_hi_page"], turn * 4 + (2 * r_ + a + 1))
                        tt(hid_lo[rows_, :, cols_], o_sum[rows_], hid_hi[rows_, :, cols_].bitcast(F32), ALU.subtract
                           ).then_inc(at["o_lo_page"], 1)

            def turn_(turn, last):
                for n in range(NU):
                    softplus(unit_of(turn, n + 2, last))
                    if n > 1 and n % PT == 1:
                        output(turn, n // PT - 1)
                    u, c, j = unit_of(turn, n, last)
                    at_ = slice(AT[j], AT[j] + W[j])
                    dve.wait_ge(at["r"], u + 1)
                    dve.wait_ge(at["mask"], u + 1)
                    tt(zb[:, c % 2, at_], zb[:, c % 2, at_], ps[:, 2 + n % 2, 0:W[j]], ALU.subtract).then_inc(at["sub"], 1)
                    capped(unit_of(turn, n + 3, last))
                    page_step(turn, n)
                output(turn, PT - 1)

            for n in range(2):
                capped((n, 0, n))
            after(dve, "rn", "maskn")
            done("subn", tt(zb_new[:], zb_new[:], zn, ALU.subtract))
            softplus((0, 0, 0))
            capped((2, 0, 2))
            softplus((1, 0, 1))
            after(dve, "on")
            for a in range(2):
                nc.vector.tensor_copy(o_new[a * HD:(a + 1) * HD].rearrange("p f b t -> p f (b t)"), sample_tiles(a)
                                      ).then_inc(at["new_out"], 1)
            turns(dve, turn_)

        def attend_pe(pe, s):
            mm = nc.tensor.matmul

            def tile_cols(n):
                return ps[:, n // (NP // 2), n % (NP // 2) * HS:(n % (NP // 2) + 1) * HS]

            def new_scores():
                pe.wait_ge(at["q_sample"], 2)
                for f in range(NP):
                    last = mm(tile_cols(NP + f)[0:TS], kT[:, f, TP:T], q_blocks[:, f].rearrange("p h b t -> p (h b t)"),
                              start=True, stop=True)
                done("zn", last)

            def new_sums():
                after(pe, "keepn")
                for c in range(2):
                    last = mm(ps[0:TS, 2 + c], tril[0:TS, 0:TS], ls_new[:, c * HB // 2:(c + 1) * HB // 2].rearrange("p h x -> p (h x)"),
                              start=True, stop=True)
                done("rn", last)

            def new_outputs():
                after(pe, "attn")
                for f in range(NP):
                    last = mm(tile_cols(f), v_tok[0:TS, PT, f * P:(f + 1) * P], zb_new[:, 2 * f:2 * f + 2].rearrange("p h x -> p (h x)"),
                              start=True, stop=True)
                done("on", last)

            def page_step(turn, n):
                r_, n = n // 8, n % 8
                if n < 4:
                    if n == 0:
                        pe.wait_ge(k_page_in, turn * 64 + 32 * (r_ + 1))
                    pe.wait_ge(k_ev[(n + 1) % 2], turn * 4 + (2 * r_ + (n + 1) // 2))
                    for f in range(NP // 2):
                        c0 = (n % 2 * (NP // 2) + f) * P
                        last = nc.tensor.transpose(ps[:, 6, f * P:(f + 1) * P], k_page[n // 2][:, c0:c0 + P], ident[:])
                    last.then_inc(at["k_tr"], 1)
                elif n == 4:
                    for m in range(2):
                        pe.wait_ge(k_ev[m], turn * 4 + (2 * r_ + 2))
                    pe.wait_ge(at["o_sum"], turn * 2 + r_)
                    for pg in range(NPG):
                        for f in range(NP):
                            c0 = (pg * NP + f) * 2 * TD
                            last = mm(ps[:, 7, c0:c0 + 2 * TD].rearrange("p (h t) -> p h t", h=2), kT_page[:, pg, f],
                                      q_blocks[:, f, :, ds(turn * 2 + r_, 1)].squeeze(2), start=True, stop=True)
                    last.then_inc(at["z_page"], 1)
                elif n == 6:
                    pe.wait_ge(at["max_page"], turn * 2 + (r_ + 1))
                    r_out = ps[:, 7, NPG * PGC:]
                    mm(r_out, tril[:], ls_page[:].rearrange("p n x -> p (n x)"), start=True, stop=False, skip_group_check=True)
                    mm(r_out[:, 0:PGC], ones[:], ls_page[:, 1], start=False, stop=False, skip_group_check=True)
                    newer = ls_new[:].rearrange("p h (b t) -> p h b t", t=TD)[:, :, ds(turn * 2 + r_, 1)].squeeze(2)
                    for pg in range(NPG):
                        last = mm(r_out[:, pg * PGC:(pg + 1) * PGC].rearrange("p (h t) -> p h t", t=TD), ones[0:TS], newer,
                                  start=False, stop=pg == NPG - 1, skip_group_check=True)
                    last.then_inc(at["r_page"], 1)
                elif n == 7:
                    pe.wait_ge(v_page_in, turn * 64 + 32 * (r_ + 1))
                    pe.wait_ge(at["att_page"], turn * 2 + (r_ + 1))
                    for pg in range(NPG):
                        for f in range(NP):
                            c = slice(f * 2 * TD, (f + 1) * 2 * TD)
                            last = mm(ps[:, 7, c], v_page[pg][:, f * P:(f + 1) * P], zb_page[:, pg, c],
                                      start=pg == 0 and f == 0, stop=pg == NPG - 1, skip_group_check=True)
                    last.then_inc(at["o_page"], 1)

            def scores(unit, turn, n):
                if unit:
                    u, c, j = unit
                    b = PT - 1 - j
                    rows_, par = slice(c % 2 * HD, (c % 2 + 1) * HD), c // 2
                    if n >= 2:
                        pe.wait_ge(at["zb"], turn * NU + (n - 1))
                    if c % 2 == 0 and j == 0:
                        pe.wait_ge(at["copied"], turn * 8 + (4 * (n // (2 * PT)) + 4))
                    mm(ps[:, 4 + j % 2, 0:W[j]], k_heads[rows_, par, b * P:(b + 1) * P], q_heads[rows_, par, b * P:],
                       start=True, stop=True).then_inc(at["z"], 1)

            def weigh(turn, n):
                u, c, j = unit_of(turn, n, True)
                a, par, b = c % 2, c // 2, PT - 1 - j
                rows_ = slice(a * HD, (a + 1) * HD)
                if j == 0:
                    if a:
                        pe.wait_ge(hid_done, turn * 2 + (s.n["hid"] + par))
                    else:
                        pe.wait_ge(at["o_lo0"], turn * 2 + par)
                pe.wait_ge(at["att"], u + 1)
                last = mm(ps[rows_, a, b * P:], v_heads[:, par, b, rows_], zb[:, a, AT[j]:AT[j] + W[j]],
                          start=j == 0, stop=j == PT - 1, skip_group_check=True)
                if j == PT - 1:
                    last.then_inc(at["o_head"], 1)

            def turn_(turn, last):
                for n in range(NU):
                    u, c, j = unit_of(turn, n, last)
                    a, bank_ = c % 2, 2 + n % 2
                    for j2 in range(j):
                        mm(ps[:, bank_, W[j] - W[j2]:W[j]], ones[:], ls[:, a, AT[j2]:AT[j2] + W[j2]],
                           start=j2 == 0, stop=False, skip_group_check=True)
                    pe.wait_ge(at["keep"], u + 1)
                    mm(ps[:, bank_, 0:W[j]], tril[:], ls[:, a, AT[j]:AT[j] + W[j]], start=j == 0, stop=True,
                       skip_group_check=True).then_inc(at["r"], 1)
                    if n:
                        weigh(turn, n - 1)
                    scores(unit_of(turn, n + 4, last), turn, n + 4)
                    page_step(turn, n)
                weigh(turn, NU - 1)

            new_scores()
            scores((0, 0, 0), 0, 0)
            scores((1, 0, 1), 0, 1)
            new_sums()
            scores((2, 0, 2), 0, 2)
            scores((3, 0, 3), 0, 3)
            new_outputs()
            pe.wait_ge(at["new_out"], 2)
            turns(pe, turn_)
            pe.wait_ge(at["o_lo_page"], 2 * NB)
            pe.wait_ge(hid_done, s.n["hid"] + KD)
        steps("at_tensor", "zn rn on")
        steps("at_vector", "zbn zcn maxn keepn maskn subn")
        steps("at_scalar", "en ln attn")

        def act_renorm(act, s, j, m):
            if s.after is not None:
                nc.scalar.activation(hx_hi[:, ds(j, 1)], xT[:, ds(j, 1)], ACT.Copy,
                                     scale=gain[:, ds(j + s.after, 1)]).then_inc(hx_hi_done, 1)
            if s.sums:
                q = KD * s.n["sum"]
                if not (isinstance(j, int) and q + j < 2):
                    act.wait_ge(ssum_done, j + (q - 1))
                nc.scalar.activation(sqb[:, m:m + 1], xT[:, ds(j, 1)], ACT.Square).then_inc(sq_done, 1)

        def dve_renorm(dve, s, j):
            if s.after is not None:
                dve.wait_ge(hx_hi_done, j + (KD * s.n["hx"] + 1))
                nc.vector.scalar_tensor_tensor(hx_lo[:, ds(j, 1)], xT[:, ds(j, 1)], gain[:, ds(j + s.after, 1)],
                                               hx_hi[:, ds(j, 1)].bitcast(F32), ALU.mult, ALU.subtract
                                               ).then_inc(hx_done, 1)

        def pool_zero(pool, s):
            if s.n["sum"]:
                pool.wait_ge(stat_done, s.n["sum"])
            nc.gpsimd.memset(ssum[:], 0.0).then_inc(ssum_zero, 1)
            pool.wait_ge(ssum_zero, s.n["sum"] + 1)

        def pool_renorm(pool, s, j, m):
            q = KD * s.n["sum"]
            pool.wait_ge(sq_done, j + (q + 1))
            if not (isinstance(j, int) and q + j == 0):
                pool.wait_ge(ssum_done, j + q)
            nc.gpsimd.tensor_tensor(ssum[:], ssum[:], sqb[:, m], ALU.add).then_inc(ssum_done, 1)

        def move_rows(eng, s, par):
            for f, (srcs, dst, i) in enumerate(s.fills):
                g = s.n["tok"] + f
                if g % 2 != par:
                    continue
                eng.wait_ge(tok_tr, g + 1)
                used = tok_uses(s, f, i)
                if used:
                    eng.wait_ge(tok_stored[i % 2], 16 * used)
                src = ps[0:dst.shape[0], 4 + g % 4]
                if par:
                    nc.scalar.activation(dst, src, ACT.Copy).then_inc(tok_ev[1], 1)
                else:
                    nc.vector.tensor_copy(dst, src).then_inc(tok_ev[0], 1)

        def tok_uses(s, f, i):
            if s.kind == "newrows" or f >= 2 * NT:
                return 0
            return i // 2 + ((NT + 1 - i % 2) // 2 if s.kind == "final" else 0)

        block = ctx.enter_context(nc.Block())
        stores = [0]

        @block.sync
        def _(sp):
            def load_unit(s, i, r):
                slot, landed = slot_of(s, r)
                u = i * 2 + r
                if not (isinstance(i, int) and unit_no(s, i, r) < 2):
                    sp.wait_ge(w_lo_done, unit_no(s, i, r) * 2 - 2)
                for dst, src in s.loads(u, slot):
                    sp.dma_start(dst, src).then_inc(landed, 16)

            def load_head(s):
                for r in range(min(2, s.units)):
                    load_unit(s, 0, r)

            def load_rest(s):
                if s.units > 4:
                    with sp.Fori(1, s.units // 2) as i:
                        load_unit(s, i, 0)
                        load_unit(s, i, 1)
                else:
                    for u in range(2, s.units):
                        load_unit(s, u // 2, u % 2)

            def store(dst, src, done=stored):
                sp.dma_start(dst, src).then_inc(done, 16)
                if done is stored:
                    stores[0] += 1

            def store_rows(s, first, prompt, sample, src=None):
                for i in range(NT):
                    g = s.n["tok"] + first + 2 * i
                    for n in (g, g + 1):
                        sp.wait_ge(tok_ev[n % 2], n // 2 + 1)
                    n = P if i < PT else TS
                    dst = prompt[i * P:(i + 1) * P] if i < PT else sample
                    if src is None:
                        store(dst, tok_out[0:n, i % 2], tok_stored[i % 2])
                    else:
                        store(dst, src[0:n, i])

            for i in range(PT):
                sp.dma_start(x_rows[:, i], A["x_prompt"][0, i * P:(i + 1) * P]).then_inc(x_in, 16)
            sp.dma_start(x_rows[0:TS, PT], A["x_sample"].rearrange("b t d -> (b t) d")).then_inc(x_in, 16)
            for name, row in (("ffn1_norm", FFN1), ("mix_norm", MIX), ("ffn2_norm", FFN2), ("ple_norm", PLE)):
                sp.dma_start(gain_rows[row:row + 2 * KD], A[name].rearrange("l (k c) -> (l k) c", c=P)).then_inc(gain_in, 16)
            for name, row in (("kv_norm", KVN), ("final_norm", FIN)):
                sp.dma_start(gain_rows[row:row + KD], A[name].rearrange("(k c) -> k c", c=P)).then_inc(gain_in, 16)
            sp.dma_start(gain_rows[ON:ON + 1], A["a_o_norm"]).then_inc(gain_in, 16)
            load_head(products[0])
            sp.dma_start(conv_rows[:], A["a_conv"][0].rearrange("j (c p) -> (j c) p", p=P)).then_inc(old_in, 16)
            sp.dma_start(old_rows[:], A["state_conv"][0].rearrange("b j c -> (b j) c")).then_inc(old_in, 16)
            sp.dma_start(bias_b[:], A["b_bias"].partition_broadcast(P)).then_inc(small_in, 16)
            sp.dma_start(pages[:], A["page_table"].rearrange("b (o n) -> o (b n)", o=1)).then_inc(small_in, 16)
            for s in plan:
                if s.units:
                    load_rest(s)
                    if following[id(s)]:
                        load_head(following[id(s)])
                elif s.kind == "p":
                    if s.layer:
                        sp.wait_ge(tile_done, 2 * s.n["unit"])
                    for i in range(PT):
                        sp.dma_start(p_rows[s.layer][:, i], A["p_prompt"][s.layer, 0, i * P:(i + 1) * P]).then_inc(p_in, 16)
                    sp.dma_start(p_rows[s.layer][0:TS, PT], A["p_sample"][s.layer].rearrange("b t d -> (b t) d")).then_inc(p_in, 16)
                elif s.kind == "newrows":
                    for par in range(2):
                        sp.wait_ge(tok_ev[par], (s.n["tok"] + len(s.fills) + 1 - par) // 2)
                    store(O["conv_prompt"][0, 0], new_rows[0:CP])
                    store(O["conv_sample"][0].rearrange("b j c -> (b j) c"), new_rows[CP:])
                elif s.kind == "gdn":
                    gdn_sp(sp, s)
                elif s.kind == "attend":
                    attend_sp(sp, s)
                elif s.kind == "kvout":
                    store_rows(s, 0, O["k_prompt"][0].rearrange("t h d -> t (h d)"), O["k_sample"].rearrange("b t h d -> (b t) (h d)"))
                    store_rows(s, 2 * NT, O["v_prompt"][0].rearrange("t h d -> t (h d)"), O["v_sample"].rearrange("b t h d -> (b t) (h d)"), v_tok)
                elif s.kind == "final":
                    store_rows(s, 0, O["y_prompt"][0], O["y_sample"].rearrange("b t d -> (b t) d"))
            sp.wait_ge(stored, 16 * stores[0])
            sp.wait_ge(s_out, 16 * HA)
            sp.wait_ge(qs_out, 32 * HA)
            for par in range(2):
                sp.wait_ge(tok_stored[par], 16 * 2 * ((NT + 1 - par) // 2))

        @block.gpsimd
        def _(pool):
            made = [0]

            def make(ins):
                made[0] += 1
                ins.then_inc(const_zero, 1)
                pool.wait_ge(const_zero, made[0])

            def select(t, op, pattern, base=0, cm=1, fill=0.0):
                make(nc.gpsimd.affine_select(out=t, in_=t, compare_op=op, fill=fill, base=base, pattern=pattern,
                                             channel_multiplier=cm))

            make(nc.gpsimd.memset(ident[:], 0.0))
            select(ident[:], ALU.not_equal, [[-1, P]], fill=1.0)
            nc.gpsimd.memset(ones[:], 1.0).then_inc(const_done, 1)
            nc.gpsimd.memset(eps[:], EPS).then_inc(const_done, 1)
            for t, sign in ((triu, 1), (tril, -1)):
                make(nc.gpsimd.memset(t[:], 1.0))
                select(t[:], ALU.is_ge, [[sign, P]], cm=-sign)
            make(nc.gpsimd.tensor_tensor(lt[:], triu[:], ident[:], ALU.subtract))
            make(nc.gpsimd.memset(same[:], 1.0))
            select(same[:], ALU.is_ge, [[-TD, NB], [0, TD]])
            select(same[:], ALU.is_ge, [[TD, NB], [0, TD]], base=TD - 1, cm=-1)
            make(nc.gpsimd.tensor_tensor(triu_s[:], triu[0:TS, 0:TS], same[:], ALU.mult))
            make(nc.gpsimd.tensor_tensor(lt_s[:], lt[0:TS, 0:TS], same[:], ALU.mult))
            for off, on in ((neg_lt, lt), (neg_le, triu), (neg_lt_s, lt_s), (neg_le_s, triu_s)):
                make(nc.gpsimd.tensor_scalar(off[:], on[:], -1.0, -NEG_BIG, ALU.add, ALU.mult))
            for level in range(7):
                b = 1 << level
                m = lm[:, level].rearrange("p (g h c) -> p g h c", h=2, c=b)
                make(nc.gpsimd.memset(lm[:, level], 0.0))
                make(nc.gpsimd.memset(m[:, :, 1], 1.0))
                groups = P // (2 * b)
                select(m[:, :, 1], ALU.is_ge, [[-2 * b, groups], [0, b]])
                select(m[:, :, 1], ALU.is_ge, [[2 * b, groups], [0, b]], base=b - 1, cm=-1)
            make(nc.gpsimd.memset(hot[:], 0.0))
            make(nc.gpsimd.memset(hot[:, 15:16], 1.0))
            make(nc.gpsimd.tensor_tensor(e32[:], ident[:, 0:32], ident[:, 32:64], ALU.add))
            make(nc.gpsimd.tensor_tensor(e32[:], e32[:], ident[:, 64:96], ALU.add))
            make(nc.gpsimd.tensor_tensor(e32[:], e32[:], ident[:, 96:128], ALU.add))
            make(nc.gpsimd.memset(a_col[:], 0.0))
            make(nc.gpsimd.memset(dt_col[:], 0.0))
            nc.gpsimd.dma_start(a_col[RB + RA:RB + RA + HA], A["a_A_log"].rearrange("o h -> h o")).then_inc(col_in, 16)
            nc.gpsimd.dma_start(dt_col[RB + RA:RB + RA + HA], A["a_dt_bias"].rearrange("o h -> h o")).then_inc(col_in, 16)

            for s in plan:
                if s.sums:
                    pool_zero(pool, s)
                if s.kind == "setup":
                    for j in range(KD):
                        pool_renorm(pool, s, j, j % 2)
                elif s.kind == "upd" and s.sums:
                    with pool.Fori(0, s.units) as u:
                        for m in range(2):
                            pool_renorm(pool, s, u * 2 + m, m)
                elif s.kind == "ple":
                    with pool.Fori(0, s.units // 2) as i:
                        for r in range(2):
                            pool_renorm(pool, s, i * 2 + r, r)
                elif s.kind == "qkv":
                    def pad(c, m):
                        nc.gpsimd.tensor_copy(seqs(xpad[:, m, CP + TP:], CP + TD)[:, :, 0:CP],
                                              seqs(old_T[:, ds(c, 1)].squeeze(1), CP)).then_inc(pad_ready, 1)

                    pool.wait_ge(setup_ev, SETUP_FILLS)
                    make(nc.gpsimd.memset(xpad[:, :, 0:CP], 0.0))
                    for m in range(2):
                        pad(m, m)

                    def keep(u, m, more):
                        pool.wait_ge(evac[m], u + (s.n["unit"] + 1))
                        c = u * 2 + m
                        new = new_T[:, ds(c, 1)].squeeze(1)
                        nc.gpsimd.tensor_copy(new[:, 0:CP], xpad[:, m, TP:TP + CP]).then_inc(new_done, 1)
                        nc.gpsimd.tensor_copy(seqs(new[:, CP:], CP), seqs(xpad[:, m, CP + TP:], CP + TD)[:, :, TD:]
                                              ).then_inc(new_done, 1)
                        if more:
                            pool.wait_ge(new_done, c * 2 + 2)
                            pool.wait_ge(tap_done, c + 1)
                            pool.wait_ge(conv_step, c * CP + CP)
                            pad(c + 2, m)
                    with pool.Fori(0, s.units - 1) as u:
                        keep(u, 0, True)
                        keep(u, 1, True)
                    keep(s.units - 1, 0, False)
                    keep(s.units - 1, 1, False)
                elif s.kind == "gdn":
                    gdn_pool(pool, s)
                elif s.kind == "attend":
                    attend_pool(pool, s)

        @block.scalar
        def _(act):
            for s in plan:
                def body(i, r, split):
                    N = unit_no(s, i, r)
                    u = i * 2 + r
                    first = isinstance(u, int) and u == 0 and s.stats
                    if s.kind == "gu":
                        split_hi(act, split, 0)
                        if first:
                            act_stats(act, s.n["stat"])
                        act.wait_ge(evac[0], N + 1)
                        if not (isinstance(u, int) and s.n["gu"] + u == 0):
                            act.wait_ge(hid_mul, u + s.n["gu"])
                        nc.scalar.activation(gate_f[:], gate_s[:], ACT.Silu).then_inc(silu_done, 1)
                        split_hi(act, split, 1)
                        act.wait_ge(hid_mul, u + (s.n["gu"] + 1))
                        nc.scalar.activation(hid_hi[:, ds(u, 1)], hid_f[:], ACT.Copy).then_inc(hid_hi_done, 1)
                    elif s.kind == "upd":
                        for m in range(2):
                            if s.after is not None or s.sums:
                                act.wait_ge(evac[m], N + 1 - m * (s.n["unit"] - s.n["eb"]))
                                act_renorm(act, s, u * 2 + m, m)
                            split_hi(act, split, m)
                    elif s.kind == "qkv":
                        for m in range(2):
                            c = u * 2 + m
                            split_hi(act, split, m)
                            if first and m == 0:
                                act_stats(act, s.n["stat"])
                            act.wait_ge(evac[m], N + 1)
                            nc.scalar.activation(cv[:, m, 0:XC], xpad[:, m, 0:XC], ACT.Copy,
                                                 scale=conv_w[:, 0, ds(c, 1)]).then_inc(tap_done, 1)
                            act.wait_ge(conv_step, c * CP + CP)
                            out = qkv[:, ds(c, 1)].squeeze(1)
                            nc.scalar.activation(out[:, 0:TP], cv[:, m, 0:TP], ACT.Silu).then_inc(conv_done, 1)
                            nc.scalar.activation(seqs(out[:, TP:T]), seqs(cv[:, m, CP + TP:], CP + TD)[:, :, 0:TD], ACT.Silu).then_inc(conv_done, 1)
                    elif s.kind == "gate":
                        for m in range(2):
                            split_hi(act, split, m)
                            act.wait_ge(evac[m], N + 1)
                            nc.scalar.activation(gates[:, ds(u * 2 + m, 1)], (gate_s, up_s)[m][:], ACT.Silu).then_inc(silu_done, 1)
                    elif s.kind == "ple":
                        split_hi(act, split, 0)
                        if first:
                            act_stats(act, s.n["stat"])
                        act.wait_ge(evac[0], N + 1)
                        act.wait_ge(evac[1], N - (s.n["unit"] - s.n["eb"]))
                        nc.scalar.activation(gate_f[:], gate_s[:], ACT.Sigmoid).then_inc(silu_done, 1)
                        split_hi(act, split, 1)
                        act.wait_ge(x_add, u + (KD * s.n["ple"] + 1))
                        act_renorm(act, s, u, r)
                    else:
                        split_hi(act, split, 0)
                        if first:
                            act_stats(act, s.n["stat"])
                        split_hi(act, split, 1)

                if s.units:
                    in_pairs(act, s, body)
                elif s.kind == "setup":
                    split_hi(act, (products[0], 0, 0), 0)
                    for k in range(KD):
                        act.wait_ge(setup_ev, k + 3)
                        act_renorm(act, s, k, k % 2)
                    split_hi(act, (products[0], 0, 0), 1)
                elif s.kind == "p":
                    act.wait_ge(p_ev, 3 * (s.layer + 1))
                    for k in range(PK):
                        nc.scalar.activation(p_hi[:, k], p_f[s.layer][:, k], ACT.Copy).then_inc(p_hi_done, 1)
                elif s.kind == "gdn":
                    gdn_act(act, s)
                elif s.kind == "attend":
                    attend_act(act, s)
                elif s.kind in ("regain", "kvout"):
                    act.wait_ge(tile_done, 2 * s.n["unit"])
                    for k in range(KD):
                        act_renorm(act, s, k, 0)
                elif s.kind == "final":
                    act_stats(act, s.n["stat"])
                move_rows(act, s, 1)


        @block.vector
        def _(dve):
            for s in plan:
                def body(i, r, split):
                    N = unit_no(s, i, r)
                    u = i * 2 + r
                    first = isinstance(u, int) and u == 0 and s.stats
                    tile_a, tile_b = N * 2 + 1, N * 2 + 2

                    def early(m):
                        if first and m == 0:
                            split_lo(dve, split, 0)
                            dve_stats(dve, s.n["stat"])

                    def late(m):
                        if not (first and m == 0):
                            split_lo(dve, split, m)

                    if s.kind == "gu":
                        dve.wait_ge(tile_done, tile_a)
                        early(0)
                        if s.n["stat"] or s.stats:
                            dve.wait_ge(rs_done, s.n["stat"] + s.stats)
                        if not (isinstance(u, int) and s.n["gs"] + u == 0):
                            dve.wait_ge(silu_done, u + s.n["gs"])
                        nc.vector.tensor_tensor(halves(gate_s[:]), TILE[0], halves(rs[:]), ALU.mult).then_inc(evac[0], 1)
                        late(0)
                        dve.wait_ge(tile_done, tile_b)
                        nc.vector.tensor_tensor(halves(up_s[:]), TILE[1], halves(rs[:]), ALU.mult).then_inc(evac[1], 1)
                        dve.wait_ge(evac[1], N + 1 - (s.n["unit"] - s.n["eb"]))
                        dve.wait_ge(silu_done, u + (s.n["gs"] + 1))
                        if not (isinstance(u, int) and s.n["gu"] + u == 0):
                            dve.wait_ge(hid_hi_done, u + s.n["hid"])
                        nc.vector.tensor_tensor(hid_f[:], gate_f[:], up_s[:], ALU.mult).then_inc(hid_mul, 1)
                        late(1)
                        dve.wait_ge(hid_hi_done, u + (s.n["hid"] + 1))
                        nc.vector.tensor_tensor(hid_lo[:, ds(u, 1)], hid_f[:].unsqueeze(1), hid_hi[:, ds(u, 1)].bitcast(F32),
                                                ALU.subtract).then_inc(hid_done, 1)
                    elif s.kind == "upd":
                        for m in range(2):
                            j = u * 2 + m
                            dve.wait_ge(tile_done, (tile_a, tile_b)[m])
                            x = halves(xT[:, ds(j, 1)].squeeze(1))
                            nc.vector.scalar_tensor_tensor(x, TILE[m], s.coef, x, ALU.mult, ALU.add).then_inc(evac[m], 1)
                            dve_renorm(dve, s, j)
                            split_lo(dve, split, m)
                    elif s.kind == "qkv":
                        for m in range(2):
                            c = u * 2 + m
                            dve.wait_ge(tile_done, (tile_a, tile_b)[m])
                            early(m)
                            dve.wait_ge(rs_done, s.n["stat"] + 1)
                            dve.wait_ge(pad_ready, c + 1)
                            at = CP + HC
                            t = TILE[m]
                            nc.vector.tensor_tensor(xpad[:, m, CP:at], t[:, 0], rs[:, 0:HC], ALU.mult)
                            nc.vector.tensor_tensor(xpad[:, m, at:CP + TP], t[:, 1, 0:TP - HC], rs[:, HC:TP], ALU.mult)
                            nc.vector.tensor_tensor(seqs(xpad[:, m, CP + TP:], CP + TD)[:, :, CP:], seqs(t[:, 1, TP - HC:]),
                                                    seqs(rs[:, TP:T]), ALU.mult).then_inc(evac[m], 1)
                            late(m)
                            dve.wait_ge(tap_done, c + 1)
                            for j in range(1, CW):
                                if j > 1:
                                    dve.wait_ge(conv_step, c * CP + j - 1)
                                nc.vector.scalar_tensor_tensor(cv[:, m, 0:XC], xpad[:, m, j:j + XC], conv_w[:, j, ds(c, 1)],
                                                               cv[:, m, 0:XC], ALU.mult, ALU.add).then_inc(conv_step, 1)
                    elif s.kind == "gate":
                        for m in range(2):
                            dve.wait_ge(tile_done, (tile_a, tile_b)[m])
                            if isinstance(u, int) and u == 0:
                                dve.wait_ge(conv_done, 2 * CT)
                            dve.wait_ge(silu_done, u * 2 + (s.n["gs"] + m - 1))
                            nc.vector.tensor_tensor(halves((gate_s, up_s)[m][:]), TILE[m], halves(rs[:]), ALU.mult
                                                    ).then_inc(evac[m], 1)
                            split_lo(dve, split, m)
                    elif s.kind == "ab":
                        dve.wait_ge(tile_done, tile_a)
                        dve.wait_ge(new_done, 2 * CT)
                        nc.vector.tensor_tensor(halves(ab[RB:P]), TILE[0][RB:P], halves(rs[RB:P]), ALU.mult).then_inc(evac[0], 1)
                        split_lo(dve, split, 0)
                        split_lo(dve, split, 1)
                    elif s.kind == "lin":
                        for m in range(2):
                            dve.wait_ge(tile_done, (tile_a, tile_b)[m])
                            early(m)
                            dve.wait_ge(rs_done, s.n["stat"] + s.stats)
                            to = halves(s.dst[:, ds(u * 2 + m, 1)].squeeze(1))
                            nc.vector.scalar_tensor_tensor(to, TILE[m], s.scale, halves(rs[:]), ALU.mult, ALU.mult
                                                           ).then_inc(evac[m], 1)
                            late(m)
                    elif s.kind == "ple":
                        dve.wait_ge(tile_done, tile_a)
                        early(0)
                        dve.wait_ge(rs_done, s.n["stat"] + 1)
                        dve.wait_ge(silu_done, u + s.n["gs"])
                        nc.vector.tensor_tensor(halves(gate_s[:]), TILE[0], halves(rs[:]), ALU.mult).then_inc(evac[0], 1)
                        late(0)
                        dve.wait_ge(tile_done, tile_b)
                        dve.wait_ge(silu_done, u + (s.n["gs"] + 1))
                        nc.vector.tensor_tensor(halves(up_s[:]), TILE[1], halves(gate_f[:]), ALU.mult).then_inc(evac[1], 1)
                        dve.wait_ge(evac[1], N + 1 - (s.n["unit"] - s.n["eb"]))
                        x = xT[:, ds(u, 1)].squeeze(1)
                        nc.vector.tensor_tensor(x, x, up_s[:], ALU.add).then_inc(x_add, 1)
                        dve_renorm(dve, s, u)
                        late(1)

                if s.units:
                    in_pairs(dve, s, body)
                elif s.kind == "setup":
                    def fill(f, dst, src):
                        dve.wait_ge(setup_tr, f + 1)
                        nc.vector.tensor_copy(dst, src).then_inc(setup_ev, 1)
                    split_lo(dve, (products[0], 0, 0), 0)
                    fill(0, gain[:], ps[:, 0, 0:10 * KD + 1])
                    fill(1, xT[:, :, TP:T], ps[:, 1].rearrange("p (k t) -> p k t", t=TS))
                    for k in range(KD):
                        fill(2 + k, xT[:, k, 0:TP], ps[:, (2 + k) % 8])
                        if k:
                            dve_renorm(dve, s, k - 1)
                    dve_renorm(dve, s, KD - 1)
                    split_lo(dve, (products[0], 0, 0), 1)
                    fill(10, conv_w[:], ps[:, 2, 0:CW * CT].rearrange("p (j c) -> p j c", c=CT))
                    for n in range(2):
                        fill(11 + n, old_T[:, 12 * n:12 * n + 12], ps[:, 3 + n, 0:12 * NB * CP].rearrange("p (c x) -> p c x", c=12))
                elif s.kind == "p":
                    for f in range(3):
                        dve.wait_ge(p_tr, 3 * s.layer + f + 1)
                        if f < 2:
                            if s.layer:
                                dve.wait_ge(p_done, PK)
                            nc.vector.tensor_copy(p_f[s.layer][:, f, 0:TP], ps[:, 4 + f]).then_inc(p_ev, 1)
                        else:
                            nc.vector.tensor_copy(p_f[s.layer][:, :, TP:T], ps[:, 6, 0:PK * TS].rearrange("p (k t) -> p k t", t=TS)
                                                  ).then_inc(p_ev, 1)
                    for k in range(PK):
                        dve.wait_ge(p_hi_done, PK * s.layer + k + 1)
                        nc.vector.tensor_tensor(p_lo[:, k], p_f[s.layer][:, k], p_hi[:, k].bitcast(F32), ALU.subtract).then_inc(p_done, 1)
                elif s.kind == "gdn":
                    gdn_dve(dve, s)
                elif s.kind == "attend":
                    attend_dve(dve, s)
                elif s.kind in ("regain", "kvout"):
                    for k in range(KD):
                        dve_renorm(dve, s, k)
                elif s.kind == "final":
                    dve_stats(dve, s.n["stat"])
                    dve.wait_ge(rs_done, s.n["stat"] + 1)
                    for k in range(KD):
                        nc.vector.scalar_tensor_tensor(yT[:, k], xT[:, k], gain[:, FIN + k:FIN + k + 1], rs[:],
                                                       ALU.mult, ALU.mult).then_inc(y_done, 1)
                move_rows(dve, s, 0)

        @block.tensor
        def _(pe):
            def transpose(dst, src):
                n = src.shape[0]
                return nc.tensor.transpose(dst, src, ident[0:n, 0:n])

            for s in plan:
                if s.units:
                    start = 0
                    if s.stats:
                        multiply(pe, s, 0, 0)
                        pe_stats(pe, s, s.n["stat"])
                        multiply(pe, s, 0, 1)
                        start = 1
                    if s.units - start > 1:
                        with pe.Fori(start, s.units) as u:
                            multiply(pe, s, u, 0)
                            multiply(pe, s, u, 1)
                    elif s.units > start:
                        multiply(pe, s, start, 0)
                        multiply(pe, s, start, 1)
                elif s.kind == "setup":
                    pe.wait_ge(const_zero, 2)
                    def fill(f, parts, *waits):
                        for w in waits:
                            pe.wait_ge(*w)
                        if f >= 8:
                            pe.wait_ge(setup_ev, f - 7)
                        for dst, src in parts:
                            last = transpose(dst, src)
                        last.then_inc(setup_tr, 1)
                    ng = 10 * KD + 1
                    fill(0, [(ps[:, 0, 0:ng], gain_rows[0:ng])], (gain_in, 16 * 7))
                    fill(1, [(ps[:, 1, k * TS:(k + 1) * TS], x_rows[0:TS, PT, k * P:(k + 1) * P]) for k in range(KD)],
                         (x_in, 16 * NT))
                    for k in range(KD):
                        fill(2 + k, [(ps[:, (2 + k) % 8, i * P:(i + 1) * P], x_rows[:, i, k * P:(k + 1) * P]) for i in range(PT)])
                    nw = CW * CT
                    fill(10, [(ps[:, 2, 0:nw], conv_rows[0:nw])], (old_in, 32))
                    no = NB * CP
                    for n in range(2):
                        fill(11 + n, [(ps[:, 3 + n, q * no:(q + 1) * no], old_rows[:, (12 * n + q) * P:(12 * n + q + 1) * P])
                                      for q in range(12)])
                elif s.kind == "p":
                    pe.wait_ge(p_in, 16 * NT * (s.layer + 1))
                    if s.layer:
                        for par in range(2):
                            pe.wait_ge(tok_ev[par], (s.n["tok"] + 1 - par) // 2)
                    else:
                        pe.wait_ge(setup_ev, SETUP_FILLS)
                    for k in range(PK):
                        for i in range(PT):
                            last = transpose(ps[:, 4 + k, i * P:(i + 1) * P], p_rows[s.layer][:, i, k * P:(k + 1) * P])
                        last.then_inc(p_tr, 1)
                    for k in range(PK):
                        last = transpose(ps[:, 6, k * TS:(k + 1) * TS], p_rows[s.layer][0:TS, PT, k * P:(k + 1) * P])
                    last.then_inc(p_tr, 1)
                elif s.kind == "gdn":
                    gdn_pe(pe, s)
                elif s.kind == "attend":
                    attend_pe(pe, s)
                elif s.kind == "final":
                    pe_stats(pe, s, s.n["stat"])
                if s.fills:
                    if s.kind == "newrows":
                        pe.wait_ge(new_done, 2 * CT)
                    elif s.kind == "kvout":
                        pe.wait_ge(evac[0], s.n["unit"])
                        pe.wait_ge(evac[1], s.n["eb"])
                    else:
                        pe.wait_ge(y_done, KD)
                    pe.wait_ge(std_done, s.n["stat"] + (s.kind == "final"))
                    pe.wait_ge(p_ev, 3 * (s.n["ple"] + (s.kind != "final" and s.kind != "kvout")))
                    for f, (srcs, dst, i) in enumerate(s.fills):
                        g = s.n["tok"] + f
                        if g >= 4:
                            pe.wait_ge(tok_ev[g % 2], (g - 4) // 2 + 1)
                        for q, src in enumerate(srcs):
                            last = transpose(ps[0:dst.shape[0], 4 + g % 4, q * P:(q + 1) * P], src)
                        last.then_inc(tok_tr, 1)


_OUTS = ["y_prompt", "y_sample", "conv_prompt", "rec_prompt", "k_prompt", "v_prompt",
         "conv_sample", "rec_sample", "k_sample", "v_sample"]


def kernel(**inputs):
    import numpy as _np
    import concourse.bacc as _bacc
    from concourse import mybir as _mybir
    from concourse.bass_utils import run_bass_kernel_spmd as _run

    nc = _bacc.Bacc("TRN2", target_bir_lowering=False, num_devices=1)
    arrays, ins = {}, {}
    for name, value in inputs.items():
        a = _np.ascontiguousarray(value)
        arrays[f"in_{name}"] = a
        ins[name] = nc.dram_tensor(f"in_{name}", a.shape, _mybir.dt.from_np(a.dtype), kind="ExternalInput").ap()
    xp, xs, st, sc = (inputs[n].shape for n in ("x_prompt", "x_sample", "state_rec", "state_conv"))
    heads = inputs["cache_k"].shape[2:]
    shapes = {
        "y_prompt": xp, "y_sample": xs,
        "conv_prompt": (st[0], xp[0]) + sc[2:], "rec_prompt": (st[0], xp[0]) + st[2:],
        "k_prompt": xp[:2] + heads, "v_prompt": xp[:2] + heads,
        "conv_sample": sc, "rec_sample": st,
        "k_sample": xs[:2] + heads, "v_sample": xs[:2] + heads,
    }
    outs = {n: nc.dram_tensor(f"out_{n}", tuple(shapes[n]), F32, kind="ExternalOutput").ap() for n in _OUTS}
    program(nc, ins, outs)
    r = _run(nc, [arrays], core_ids=[0])
    return tuple(r.results[0][f"out_{n}"] for n in _OUTS)
```
